# Optimizing a Trainium2 kernel written in Bass

```python
import math
import jax, jax.numpy as jnp
from jax import lax
import numpy as np

D_MODEL = 2048
BATCH = 1
SEQ = 256
DEPTH = 1
DEC_BATCH = 8
DEC_SEQ = 1
PAST_LEN = 2048
PAGE_SIZE = 128

A_HEADS = 4
A_DK = 128
A_DV = 128
A_WIDTH = A_HEADS * A_DV
B_HEADS = 8
B_DK = 128
B_DV = 128
B_WIDTH = B_HEADS * B_DV
C_BLOCKS = 8
C_WIDTH = 512
C_BLOCK = C_WIDTH // C_BLOCKS
RG_C = 8.0
CONV_W = 4
MIX_WIDTH = A_WIDTH + B_WIDTH + C_WIDTH
D_FF = -(-8 * D_MODEL // (3 * 256)) * 256
CHUNK = 64
NORM_EPS = 1e-6
L2_EPS = 1e-6
IN_SIZES = (A_HEADS * A_DK, A_HEADS * A_DK, A_WIDTH, A_WIDTH,
            B_HEADS * B_DK, B_HEADS * B_DK, B_WIDTH, B_WIDTH,
            B_HEADS, B_HEADS,
            C_WIDTH, C_WIDTH)
IN_TOTAL = sum(IN_SIZES)

kernel_name = "hybrid_hgrn2_gdn_rglru_decode_step"

def _split_points():
    pts, acc = [], 0
    for s in IN_SIZES[:-1]:
        acc += s
        pts.append(acc)
    return pts

def rmsnorm(x, g):
    xf = x.astype(jnp.float32)
    return xf * lax.rsqrt(jnp.mean(xf * xf, axis=-1, keepdims=True) + NORM_EPS) * g.astype(jnp.float32)

def l2norm(x):
    return x * lax.rsqrt(jnp.sum(x * x, axis=-1, keepdims=True) + L2_EPS)

def causal_dwconv(x, buf, w, b):
    L = x.shape[1]
    xc = jnp.concatenate([buf.astype(jnp.float32), x], axis=1)
    w = w.astype(jnp.float32)
    y = w[0] * xc[:, 0:L]
    for j in range(1, CONV_W):
        y = y + w[j] * xc[:, j:j + L]
    if b is not None:
        y = y + b.astype(jnp.float32)
    return y, xc[:, L:]

def _to_chunks(t, C):
    Bn, L, H, d = t.shape
    return t.reshape(Bn, L // C, C, H, d).transpose(1, 0, 3, 2, 4)

def _from_chunks(o):
    n, Bn, H, C, e = o.shape
    return o.transpose(1, 0, 3, 2, 4).reshape(Bn, n * C, H, e)

def hgrn2_chunked(q, logf, v, S0):
    L = q.shape[1]
    C = math.gcd(L, CHUNK)
    k = -jnp.expm1(logf)
    qc, kc, vc, lc = (_to_chunks(t, C) for t in (q, k, v, logf))
    causal = jnp.tril(jnp.ones((C, C), dtype=bool))

    def step(S, inp):
        qi, ki, vi, li = inp
        b = jnp.cumsum(li, axis=-2)
        rel = b[..., :, None, :] - b[..., None, :, :]
        dec = jnp.exp(jnp.where(causal[:, :, None], rel, -jnp.inf))
        att = jnp.einsum('bhtd,bhsd,bhtsd->bhts', qi, ki, dec)
        o = (jnp.einsum('bhts,bhse->bhte', att, vi)
             + jnp.einsum('bhtd,bhde->bhte', qi * jnp.exp(b), S))
        b_last = b[..., -1:, :]
        S_new = (jnp.exp(b_last[..., 0, :])[..., None] * S
                 + jnp.einsum('bhsd,bhse->bhde', ki * jnp.exp(b_last - b), vi))
        return S_new, o

    S, o = lax.scan(step, S0, (qc, kc, vc, lc))
    return _from_chunks(o), S

def gated_delta_chunked(q, k, v, g, beta, S0):
    L = q.shape[1]
    DV = v.shape[-1]
    C = math.gcd(L, CHUNK)
    qc, kc, vc, gc, bc = (_to_chunks(t, C) for t in (q, k, v, g[..., None], beta[..., None]))
    causal = jnp.tril(jnp.ones((C, C), dtype=bool))
    strict = jnp.tril(jnp.ones((C, C), dtype=bool), -1)
    eye = jnp.eye(C, dtype=jnp.float32)

    def step(S, inp):
        qi, ki, vi, gi, bi = inp
        b = jnp.cumsum(gi[..., 0], axis=-1)
        gam = jnp.exp(jnp.where(causal, b[..., :, None] - b[..., None, :], -jnp.inf))
        A = jnp.where(strict, bi * jnp.einsum('bhtd,bhsd->bhts', ki, ki) * gam, 0.0)
        rhs = jnp.concatenate([bi * vi, bi * ki * jnp.exp(b)[..., None]], axis=-1)
        sol = lax.linalg.triangular_solve(eye + A, rhs, left_side=True, lower=True, unit_diagonal=True)
        u = sol[..., :DV] - jnp.einsum('bhtd,bhde->bhte', sol[..., DV:], S)
        qk = jnp.einsum('bhtd,bhsd->bhts', qi, ki) * gam
        o = (jnp.einsum('bhtd,bhde->bhte', qi * jnp.exp(b)[..., None], S)
             + jnp.einsum('bhts,bhse->bhte', qk, u))
        S_new = (jnp.exp(b[..., -1])[..., None, None] * S
                 + jnp.einsum('bhsd,bhse->bhde', ki * jnp.exp(b[..., -1:] - b)[..., None], u))
        return S_new, o

    S, o = lax.scan(step, S0, (qc, kc, vc, gc, bc))
    return _from_chunks(o), S

def _lin_combine(e1, e2):
    a1, b1 = e1
    a2, b2 = e2
    return a1 * a2, a2 * b1 + b2

def rglru(x, h0, w_a, b_a, w_x, b_x, lam, seq_start):
    Bn, L, _ = x.shape
    xb = x.reshape(Bn, L, C_BLOCKS, C_BLOCK)
    r = jax.nn.sigmoid(jnp.einsum('blni,nij->blnj', xb, w_a).reshape(Bn, L, C_WIDTH) + b_a)
    i = jax.nn.sigmoid(jnp.einsum('blni,nij->blnj', xb, w_x).reshape(Bn, L, C_WIDTH) + b_x)
    log_a = -RG_C * r * jax.nn.softplus(-lam.astype(jnp.float32))
    a = jnp.exp(log_a)
    mult = jnp.sqrt(-jnp.expm1(2.0 * log_a))
    if seq_start:
        mult = mult.at[:, 0].set(1.0)
    A_cum, B_cum = lax.associative_scan(_lin_combine, (a, mult * (i * x)), axis=1)
    h = B_cum + A_cum * h0[:, None, :]
    return h, h[:, -1]

def layer(x, S_a, S_b, buf_b, h_c, buf_c, lb, seq_start, prm):
    (g_mix_pre, g_mix_post, g_ffn_pre, g_ffn_post, w_in, w_out, a_norm,
     b_conv_w, b_A_log, b_dt_bias, b_norm, c_conv_w, c_conv_b, c_wa, c_ba, c_wx, c_bx, c_lam,
     w_gate, w_up, w_down) = prm
    f32 = jnp.float32
    Bn, L, _ = x.shape
    h = rmsnorm(x, g_mix_pre)
    proj = jnp.einsum('bld,de->ble', h, w_in)
    (aq, af, ai, ag, bq, bk, bv, bz, bb, ba, cx, cg) = jnp.split(proj, _split_points(), axis=-1)

    qa = jax.nn.silu(aq).reshape(Bn, L, A_HEADS, A_DK)
    lbf = lb.astype(f32)
    logf = jnp.logaddexp(jnp.log(lbf), jnp.log1p(-lbf) + jax.nn.log_sigmoid(af))
    oa, S_a_new = hgrn2_chunked(qa, logf.reshape(Bn, L, A_HEADS, A_DK),
                                ai.reshape(Bn, L, A_HEADS, A_DV), S_a.astype(f32))
    oa = (rmsnorm(oa, a_norm) * jax.nn.silu(ag.reshape(Bn, L, A_HEADS, A_DV))).reshape(Bn, L, A_WIDTH)

    qkv, buf_b_new = causal_dwconv(jnp.concatenate([bq, bk, bv], axis=-1), buf_b, b_conv_w, None)
    qb, kb, vb = jnp.split(jax.nn.silu(qkv), 3, axis=-1)
    qb = l2norm(qb.reshape(Bn, L, B_HEADS, B_DK)) * (B_DK ** -0.5)
    kb = l2norm(kb.reshape(Bn, L, B_HEADS, B_DK))
    vb = vb.reshape(Bn, L, B_HEADS, B_DV)
    beta = jax.nn.sigmoid(bb)
    gdec = -jnp.exp(b_A_log.astype(f32)) * jax.nn.softplus(ba + b_dt_bias)
    ob, S_b_new = gated_delta_chunked(qb, kb, vb, gdec, beta, S_b.astype(f32))
    ob = (rmsnorm(ob, b_norm) * jax.nn.silu(bz.reshape(Bn, L, B_HEADS, B_DV))).reshape(Bn, L, B_WIDTH)

    xcv, buf_c_new = causal_dwconv(cx, buf_c, c_conv_w, c_conv_b)
    hc, h_c_new = rglru(xcv, h_c.astype(f32), c_wa, c_ba, c_wx, c_bx, c_lam, seq_start)
    oc = hc * jax.nn.gelu(cg)

    mix = jnp.einsum('ble,ed->bld', jnp.concatenate([oa, ob, oc], axis=-1), w_out)
    x = x + rmsnorm(mix, g_mix_post).astype(x.dtype)
    h2 = rmsnorm(x, g_ffn_pre)
    ff = jnp.einsum('blf,fd->bld', jax.nn.silu(h2 @ w_gate) * (h2 @ w_up), w_down)
    x = x + rmsnorm(ff, g_ffn_post).astype(x.dtype)
    return x, (S_a_new, S_b_new, buf_b_new, h_c_new, buf_c_new)

def setup_inputs(seed: int = 0) -> dict:
    key = jax.random.key(seed)
    keys = jax.random.split(key, 40)
    cnt = [0]
    f32 = jnp.float32

    def nk():
        k = keys[cnt[0]]
        cnt[0] += 1
        return k

    def nrm(shape, s):
        return s * jax.random.normal(nk(), shape, f32)

    def gain(shape):
        return 1.0 + 0.05 * jax.random.normal(nk(), shape, f32)

    x_prompt = nrm((BATCH, SEQ, D_MODEL), 1.0)
    x_sample = nrm((DEC_BATCH, DEC_SEQ, D_MODEL), 1.0)
    state_hgrn = nrm((DEPTH, DEC_BATCH, A_HEADS, A_DK, A_DV), 0.5)
    state_gdn = nrm((DEPTH, DEC_BATCH, B_HEADS, B_DK, B_DV), 0.5)
    state_gdn_conv = nrm((DEPTH, DEC_BATCH, CONV_W - 1, 3 * B_WIDTH), 1.0)
    state_rglru_h = nrm((DEPTH, DEC_BATCH, C_WIDTH), 0.5)
    state_rglru_conv = nrm((DEPTH, DEC_BATCH, CONV_W - 1, C_WIDTH), 1.0)
    ln_mix_pre = gain((DEPTH, D_MODEL))
    ln_mix_post = gain((DEPTH, D_MODEL))
    ln_ffn_pre = gain((DEPTH, D_MODEL))
    ln_ffn_post = gain((DEPTH, D_MODEL))
    w_in = nrm((DEPTH, D_MODEL, IN_TOTAL), D_MODEL ** -0.5)
    w_out = nrm((DEPTH, MIX_WIDTH, D_MODEL), MIX_WIDTH ** -0.5)
    a_lb_logits = nrm((DEPTH, A_HEADS * A_DK), 0.5)
    a_norm = gain((DEPTH, A_DV))
    b_conv_w = nrm((DEPTH, CONV_W, 3 * B_WIDTH), CONV_W ** -0.5)
    b_A_log = jnp.log(jax.random.uniform(nk(), (DEPTH, B_HEADS), f32, 1.0, 16.0))
    dt = jnp.exp(jax.random.uniform(nk(), (DEPTH, B_HEADS), f32, math.log(1e-3), math.log(1e-1)))
    b_dt_bias = dt + jnp.log(-jnp.expm1(-dt))
    b_norm = gain((DEPTH, B_DV))
    c_conv_w = nrm((DEPTH, CONV_W, C_WIDTH), CONV_W ** -0.5)
    c_conv_b = nrm((DEPTH, C_WIDTH), 0.02)
    c_wa = nrm((DEPTH, C_BLOCKS, C_BLOCK, C_BLOCK), C_BLOCK ** -0.5)
    c_ba = nrm((DEPTH, C_WIDTH), 0.1)
    c_wx = nrm((DEPTH, C_BLOCKS, C_BLOCK, C_BLOCK), C_BLOCK ** -0.5)
    c_bx = nrm((DEPTH, C_WIDTH), 0.1)
    u = jax.random.uniform(nk(), (DEPTH, C_WIDTH), f32, 0.9, 0.999)
    a_base = u ** (1.0 / RG_C)
    c_lam = jnp.log(a_base) - jnp.log1p(-a_base)
    w_gate = nrm((DEPTH, D_MODEL, D_FF), D_MODEL ** -0.5)
    w_up = nrm((DEPTH, D_MODEL, D_FF), D_MODEL ** -0.5)
    w_down = nrm((DEPTH, D_FF, D_MODEL), D_FF ** -0.5)
    return {"x_prompt": x_prompt, "x_sample": x_sample,
            "state_hgrn": state_hgrn, "state_gdn": state_gdn, "state_gdn_conv": state_gdn_conv,
            "state_rglru_h": state_rglru_h, "state_rglru_conv": state_rglru_conv,
            "ln_mix_pre": ln_mix_pre, "ln_mix_post": ln_mix_post,
            "ln_ffn_pre": ln_ffn_pre, "ln_ffn_post": ln_ffn_post,
            "w_in": w_in, "w_out": w_out, "a_lb_logits": a_lb_logits, "a_norm": a_norm,
            "b_conv_w": b_conv_w, "b_A_log": b_A_log, "b_dt_bias": b_dt_bias, "b_norm": b_norm,
            "c_conv_w": c_conv_w, "c_conv_b": c_conv_b, "c_wa": c_wa, "c_ba": c_ba,
            "c_wx": c_wx, "c_bx": c_bx, "c_lam": c_lam,
            "w_gate": w_gate, "w_up": w_up, "w_down": w_down}

def reference(x_prompt, x_sample, state_hgrn, state_gdn, state_gdn_conv, state_rglru_h, state_rglru_conv,
              ln_mix_pre, ln_mix_post, ln_ffn_pre, ln_ffn_post, w_in, w_out, a_lb_logits, a_norm,
              b_conv_w, b_A_log, b_dt_bias, b_norm, c_conv_w, c_conv_b, c_wa, c_ba, c_wx, c_bx, c_lam,
              w_gate, w_up, w_down):
    f32 = jnp.float32
    lbs = jnp.cumsum(jax.nn.softmax(a_lb_logits.astype(f32), axis=0), axis=0)
    lbs = lbs - lbs[0:1]
    xp, xs = x_prompt, x_sample
    Bp = x_prompt.shape[0]
    new_p, new_s = [], []
    for l in range(DEPTH):
        prm = (ln_mix_pre[l], ln_mix_post[l], ln_ffn_pre[l], ln_ffn_post[l], w_in[l], w_out[l], a_norm[l],
               b_conv_w[l], b_A_log[l], b_dt_bias[l], b_norm[l], c_conv_w[l], c_conv_b[l],
               c_wa[l], c_ba[l], c_wx[l], c_bx[l], c_lam[l], w_gate[l], w_up[l], w_down[l])
        xp, sp = layer(xp,
                       jnp.zeros((Bp, A_HEADS, A_DK, A_DV), f32),
                       jnp.zeros((Bp, B_HEADS, B_DK, B_DV), f32),
                       jnp.zeros((Bp, CONV_W - 1, 3 * B_WIDTH), f32),
                       jnp.zeros((Bp, C_WIDTH), f32),
                       jnp.zeros((Bp, CONV_W - 1, C_WIDTH), f32),
                       lbs[l], True, prm)
        xs, ss = layer(xs, state_hgrn[l], state_gdn[l], state_gdn_conv[l], state_rglru_h[l],
                       state_rglru_conv[l], lbs[l], False, prm)
        new_p.append(sp)
        new_s.append(ss)

    def stk(lst, i, dt):
        return jnp.stack([s[i] for s in lst], axis=0).astype(dt)

    return (xp, xs,
            stk(new_p, 0, state_hgrn.dtype), stk(new_s, 0, state_hgrn.dtype),
            stk(new_p, 1, state_gdn.dtype), stk(new_s, 1, state_gdn.dtype),
            stk(new_p, 2, state_gdn_conv.dtype), stk(new_s, 2, state_gdn_conv.dtype),
            stk(new_p, 3, state_rglru_h.dtype), stk(new_s, 3, state_rglru_h.dtype),
            stk(new_p, 4, state_rglru_conv.dtype), stk(new_s, 4, state_rglru_conv.dtype))


_drawn_inputs = setup_inputs


def setup_inputs(seed=0):
    import zlib

    import numpy as np

    out = dict(_drawn_inputs(seed))
    spreads = {}
    factors = {}
    for name, (base, spread) in spreads.items():
        noise = np.random.default_rng([zlib.crc32(name.encode()), seed]).standard_normal(out[name].shape)
        drawn = base * np.exp(spread * noise) if base else spread * noise
        out[name] = __import__('jax').numpy.asarray(drawn.astype(out[name].dtype))
    for name, factor in factors.items():
        out[name] = (out[name] * factor).astype(out[name].dtype)
    return out
```

```python
from contextlib import ExitStack
from math import log

import concourse.bass as bass
from concourse import mybir

F32 = mybir.dt.float32
F32R = mybir.dt.float32r
ALU = mybir.AluOpType
ACT = mybir.ActivationFunctionType
AX = mybir.AxisListType
ds = bass.ds

P = 128
L = 256
NB = 8
T = L + NB
D = 2048
KT = D // P
FF = 5632
FT = FF // P
EPS = 1e-6
CK = 4
CC = 256
RING = 4
AHEAD = RING - 1
SLOTS = 16
GATE_OFF = 6144
C_OFF = 6160
LEVELS = 7
CONVW = 4
XW = 3 + L + NB * CONVW
CW = XW - 3
B_ROUNDS, A_ROUNDS = 4, 2
ROUNDS = B_ROUNDS + A_ROUNDS + 1
OUT_GROUPS, FF_PAIRS, DOWN_GROUPS = 8, 22, 8
OUT_C0 = ROUNDS * SLOTS
FF_C0 = OUT_C0 + OUT_GROUPS * 4
DOWN_C0 = FF_C0 + FF_PAIRS * 8
DOWN_CH = FT // CK
CHUNKS = DOWN_C0 + DOWN_GROUPS * DOWN_CH
OUT_START = [(0, 1), (0, 2), (1, 1), (1, 2), (0, 0), (1, 0), (0, 3), (1, 3)]
OUT_G0, FF_G0, DOWN_G0 = 28, 36, 80
G_MIX_PRE, G_MIX_POST, G_FFN_PRE, G_FFN_POST, RG_H, C_CONV = 0, 16, 32, 48, 64, 96
B_CONV, C_BIAS, C_BA, C_BX, C_LAM, A_NORM, B_NORM, C_HIST = 112, 208, 212, 216, 220, 224, 225, 226
PCOLS = 322
F_B, F_BETA, F_BETAEXP, F_KEND, F_EEND, F_G = range(6)
SERIES = [1 / 15, 1 / 13, 1 / 11, 1 / 9, 1 / 7, 1 / 5, 1 / 3, 1.0]


def hybrid_layer(nc, x_prompt, x_sample, state_hgrn, state_gdn, state_gdn_conv, state_rglru_h, state_rglru_conv,
                 ln_mix_pre, ln_mix_post, ln_ffn_pre, ln_ffn_post, w_in, w_out, a_norm,
                 b_conv_w, b_A_log, b_dt_bias, b_norm, c_conv_w, c_conv_b, c_wa, c_ba, c_wx, c_bx, c_lam,
                 w_gate, w_up, w_down,
                 y_prompt, y_sample, o_hgrn_p, o_hgrn_s, o_gdn_p, o_gdn_s, o_gconv_p, o_gconv_s,
                 o_rh_p, o_rh_s, o_rconv_p, o_rconv_s):
    with ExitStack() as ctx:
        at = [16640]
        place = {}

        def put(name, shape, dt=F32, offset=None):
            size = 4
            for s in shape[1:]:
                size *= s
            if offset is None:
                offset = at[0]
                at[0] += -(-size // 32) * 32
            assert offset + size <= 229368, (name, offset + size)
            place[name] = offset
            return nc.alloc_sbuf_tensor_at(name, [*shape], dt, offset=offset)

        def sem(name):
            return ctx.enter_context(nc.semaphore(name))

        xT = put("xT", [P, KT, T])
        act_hi = put("act_hi", [P, KT, T], F32R)
        act_lo = put("act_lo", [P, KT, T], F32R)
        raw = put("raw", [P, RING, CK, CC])
        w_hi = put("w_hi", [P, RING, CK, CC], F32R)
        w_lo = put("w_lo", [P, RING, CK, CC], F32R)
        masks = put("masks", [P, 1 + LEVELS, P])
        upper = put("upper", [P, P])
        ones = put("ones", [P, P])
        params = put("params", [P, PCOLS])
        consts = put("consts", [P, 4])
        rbc = put("rbc", [P, T])
        ident = masks[:, 0, :]
        eps = consts[:, 0:1]

        overlay = at[0]
        cat_hi = put("cat_hi", [P, KT, T], F32R)
        cat_lo = put("cat_lo", [P, KT, T], F32R)
        qkv = put("qkv", [P, 4, 2, T])
        xraw = put("xraw", [P, 2, 2, XW])
        conv = put("conv", [P, 2, CW])
        convw = put("convw", [P, 2, 2, CONVW])
        tail_b = put("tail_b", [P, 3 + NB, 24])
        tail_c = put("tail_c", [P, 11 + 9, 4])
        hist_b = put("hist_b", [P, NB, 3, 24])
        gates = put("gates", [P, 6, 4, 4])
        sgates = put("sgates", [P, 2, 4, 16])
        lamc = put("lamc", [P, 2, 4])
        pair = put("pair", [P, 6, 4])
        spair = put("spair", [P, 2, 16])
        small = put("small", [P, 6, 16])
        S = put("S", [P, 2, 2, P])
        sq = put("sq", [P, 4, T])
        rs = put("rs", [P, 4, T])
        nrm = put("nrm", [P, 2, 2, T])
        oT = put("oT", [P, 2, T])
        nwT = put("nwT", [P, 2, P])
        decay = put("decay", [P, 4, P])
        eb = put("eb", [P, 4, P])
        kb = put("kb", [P, 4, P])
        k_end = put("k_end", [P, 4, P])
        kbe = put("kbe", [P, 4, P])
        vb = put("vb", [P, 4, P])
        AT = put("AT", [P, 4, P])
        QK = put("QK", [P, 4, P])
        TT = put("TT", [P, 4, P])
        u = put("u", [P, 4, P])
        Ss = put("Ss", [P, 16, P])
        sqv = sq[:, :, :].rearrange("p a t -> p (a t)")
        rsv = rs[:, :, :].rearrange("p a t -> p (a t)")
        AL = sqv[:, 0:512].rearrange("p (x t) -> p x t", x=4)
        XM = rsv[:, 0:512].rearrange("p (x t) -> p x t", x=4)
        TM = rsv[:, 512:1024].rearrange("p (x t) -> p x t", x=4)
        lev = put("lev", [P, LEVELS, 512], offset=place["decay"])
        prod = sqv[:, 0:1024].rearrange("p (l t) -> p l t", l=8)
        attT = TT
        qA = u[:, :, :].rearrange("p (j c) t -> p j (c t)", j=2)
        q_s = small[:, 2, :]
        bA = sqv[:, 0:512].rearrange("p (x t) -> p x t", x=4)
        kend_f = sqv[:, 512:1024].rearrange("p (x t) -> p x t", x=4)
        v_tm = rsv[:, 0:512].rearrange("p (x t) -> p x t", x=4)
        ke_tm = rsv[:, 512:1024].rearrange("p (x t) -> p x t", x=4)
        ca = put("ca", [P, 4, T], offset=place["decay"])
        cth = put("cth", [P, 4, T], offset=place["decay"] + 4 * 4 * T)
        cm = put("cm", [P, 4, T], offset=place["decay"] + 8 * 4 * T)
        wbd = put("wbd", [P, 2, 4, P])
        xtok = put("xtok", [P, 3, D], offset=place["qkv"])
        hF = put("hF", [P, KT, T], offset=place["cat_hi"])
        stage = put("stage", [P, 8, P], offset=place["u"])
        bab = put("bab", [16, T], offset=place["decay"])
        gw = put("gw", [P, KT, 16], offset=place["cat_lo"])
        gt = put("gt", [P, 3, 16], offset=place["decay"] + 2048)
        zz = put("zz", [P, 6, 28], offset=place["decay"] + 2304)
        sel = put("sel", [8, 2, 8, 8], offset=place["decay"] + 3072)
        bcA = put("bcA", [P, 8], offset=place["decay"] + 3648)
        bcD = put("bcD", [P, 8], offset=place["decay"] + 3680)
        gb = put("gb", [P, 2, 16], offset=place["decay"] + 3712)
        mixg = put("mixg", [P, KT, T], offset=place["decay"])
        rows = put("rows", [P, 4, P], offset=place["sq"])
        hid_hi = put("hid_hi", [P, FT, T], F32R, offset=overlay)
        hid_lo = put("hid_lo", [P, FT, T], F32R, offset=overlay + FT * T * 4)
        after = overlay + 2 * FT * T * 4
        sqo = put("sqo", [P, 2, 2, T], offset=after)
        sgate = put("sgate", [P, 2, T], offset=after + 16 * T)
        hidF = put("hidF", [P, 2, T], offset=after + 24 * T)
        ffg = put("ffg", [P, KT, T], offset=place["act_lo"])
        ytok = put("ytok", [P, 3, D], offset=overlay)

        ps = ctx.enter_context(nc.psum_tensor("ps", [P, 8, 512], F32))

        def acc(par):
            return ps[:, 2 * par:2 * par + 2, 0:T]

        def quad(bank):
            return ps[:, bank, :].rearrange("p (x t) -> p x t", x=4)

        raw_in = [sem(f"raw_in{i}") for i in range(RING)]
        hi_done = sem("hi_done")
        lo_done = sem("lo_done")
        pe_used = sem("pe_used")
        drained = [sem("drained0"), sem("drained1")]
        g_done = sem("g_done")
        raw_q = sem("raw_q")
        hist_in = sem("hist_in")
        conv_done = sem("conv_done")
        silu_done = sem("silu_done")
        x_in = sem("x_in"); par_in = sem("par_in"); gw_in = sem("gw_in"); bc_in = sem("bc_in"); wbd_in = sem("wbd_in")
        pool_c = sem("pool_c"); st_pe = sem("st_pe"); st_dve = sem("st_dve"); st_act = sem("st_act")
        nz_pe = sem("nz_pe"); nz_sq = sem("nz_sq"); nz_r = sem("nz_r"); nz_h = sem("nz_h"); nz_hi = sem("nz_hi"); nz_lo = sem("nz_lo")
        mx = {n: sem("mx_" + n) for n in (
            "pair", "sq", "ss", "ln", "rs", "nrm", "bc", "tr", "eb", "kb", "d", "dec", "cau", "tm", "qe", "g", "at",
            "al", "tt", "t1", "t", "x", "xc", "p", "u0", "u0c", "s1", "s1c", "u1", "u1c", "so", "s2", "oc",
            "ks", "qkp", "qk", "us", "sdec", "ub", "sn", "os", "osq", "oss", "oln", "ors", "og", "ohi", "olo",
            "ld", "st")}
        a_ = {n: sem("ha_" + n) for n in (
            "k", "ln", "lf", "b", "d", "ab", "e", "ex", "w", "tr", "tm", "at", "pr", "rd", "fs", "vs", "q")}
        c_ = {n: sem("rg_" + n) for n in ("pre", "r", "prei", "i", "a", "x", "h", "hi", "lo")}
        o_pe = sem("o_pe"); o_sq = sem("o_sq"); o_r = sem("o_r"); o_y = sem("o_y"); o_g = sem("o_g")
        tl_pe = sem("tl_pe"); tl_cp = sem("tl_cp"); tl_out = sem("tl_out"); old_out = sem("old_out")
        o_pool = sem("o_pool")
        gate_act = sem("gate_act"); gate_r = sem("gate_r"); ff_hi = sem("ff_hi")
        y_pe = sem("y_pe"); y_cp = sem("y_cp"); y_out = sem("y_out")

        block = ctx.enter_context(nc.Block())

        @block.sync
        def _(sp):
            w_in_v = w_in[0].rearrange("(k p) n -> p k n", p=P)
            w_out_v = w_out[0].rearrange("(k p) n -> p k n", p=P)
            w_gate_v = w_gate[0].rearrange("(k p) n -> p k n", p=P)
            w_up_v = w_up[0].rearrange("(k p) n -> p k n", p=P)
            w_down_v = w_down[0].rearrange("(k p) n -> p k n", p=P)

            def load(c, slot, src, first=False):
                if not first:
                    sp.wait_ge(lo_done, c - RING + 1)
                sp.dma_start(raw[:, slot], src).then_inc(raw_in[slot], 16)

            def in_group(c0, col, first=False):
                for i in range(4):
                    load(c0 + i, i, w_in_v[:, 4 * i:4 * i + 4, col], first)

            for t in range(2):
                sp.dma_start(xtok[:, t], x_prompt[0, t * P:(t + 1) * P, :]).then_inc(x_in, 16)
            sp.dma_start(xtok[0:NB, 2], x_sample[:, 0, :]).then_inc(x_in, 16)
            for n, a in enumerate((ln_mix_pre, ln_mix_post, ln_ffn_pre, ln_ffn_post)):
                sp.dma_start(stage[16 * n:16 * n + 16, 0], a.rearrange("o (k p) -> (o k) p", p=P)).then_inc(par_in, 16)
            sp.dma_start(stage[64:96, 0], state_rglru_h[0].rearrange("b (k p) -> (b k) p", p=P)).then_inc(par_in, 16)
            sp.dma_start(stage[96:112, 0], c_conv_w[0].rearrange("j (k p) -> (j k) p", p=P)).then_inc(par_in, 16)
            sp.dma_start(stage[0:96, 1], b_conv_w[0].rearrange("j (k p) -> (j k) p", p=P)).then_inc(par_in, 16)
            for n, a in enumerate((c_conv_b, c_ba, c_bx, c_lam)):
                sp.dma_start(stage[96 + 4 * n:100 + 4 * n, 1], a.rearrange("o (k p) -> (o k) p", p=P)).then_inc(par_in, 16)
            sp.dma_start(stage[112:113, 1], a_norm).then_inc(par_in, 16)
            sp.dma_start(stage[113:114, 1], b_norm).then_inc(par_in, 16)
            sp.dma_start(stage[0:96, 2], state_rglru_conv[0].rearrange("b j (k p) -> (b j k) p", p=P)).then_inc(par_in, 16)
            hist = state_gdn_conv[0].rearrange("b j (k p) -> (b j k) p", p=P)
            for n in range(4):
                sp.dma_start(stage[:, 3 + n], hist[P * n:P * n + P, :]).then_inc(par_in, 16)
            sp.dma_start(stage[0:64, 7], hist[512:576, :]).then_inc(par_in, 16)
            sp.dma_start(gw[:, :, :], w_in_v[:, :, GATE_OFF:GATE_OFF + 16]).then_inc(gw_in, 16)
            sp.dma_start(bcA[:, :], b_A_log.broadcast_to([P, 8])).then_inc(bc_in, 16)
            sp.dma_start(bcD[:, :], b_dt_bias.broadcast_to([P, 8])).then_inc(bc_in, 16)
            b_col = [2048, 3072, 4096, 5120]
            for q in range(4):
                in_group(4 * q, slice(b_col[q], b_col[q] + CC), first=(q == 0))
            with sp.Fori(1, B_ROUNDS) as r:
                for q in range(4):
                    in_group(SLOTS * r + 4 * q, ds(r * CC + b_col[q], CC))
            for r in range(A_ROUNDS):
                for q in range(4):
                    in_group(SLOTS * (B_ROUNDS + r) + 4 * q, slice(512 * q + CC * r, 512 * q + CC * r + CC))
            for q in range(4):
                in_group(SLOTS * (ROUNDS - 1) + 4 * q, slice(C_OFF + CC * q, C_OFF + CC * q + CC))
            for s, (g, i) in enumerate(OUT_START):
                load(OUT_C0 + s, s % RING, w_out_v[:, 4 * i:4 * i + 4, g * CC:g * CC + CC])
            with sp.Fori(2, OUT_GROUPS) as g:
                for i in range(4):
                    load(4 * g + OUT_C0 + i, i, w_out_v[:, 4 * i:4 * i + 4, ds(g * CC, CC)])
            with sp.Fori(0, FF_PAIRS) as g:
                for n, w in enumerate((w_gate_v, w_up_v)):
                    for i in range(4):
                        load(8 * g + FF_C0 + 4 * n + i, i, w[:, 4 * i:4 * i + 4, ds(g * CC, CC)])
            with sp.Fori(0, 2) as h:
                for g in range(4):
                    for i in range(DOWN_CH):
                        c = DOWN_CH * g + i
                        load(44 * h + DOWN_C0 + c, c % RING, w_down_v[:, CK * i:CK * i + CK, ds(h * 1024 + g * CC, CC)])
            for t in range(3):
                n = P if t < 2 else NB
                dst = y_prompt[0, t * P:(t + 1) * P, :] if t < 2 else y_sample[:, 0, :]
                sp.wait_ge(y_cp, 4 * t + 4)
                sp.dma_start(dst, ytok[0:n, t]).then_inc(y_out, 16)
            sp.wait_ge(y_out, 48)

        @block.gpsimd
        def _(pool):
            steps = [0]
            passed = sem("passed")

            def const(ins):
                ins.then_inc(pool_c, 1)
                steps[0] += 1
                pool.wait_ge(pool_c, steps[0])

            const(pool.memset(masks[:, :, :], 0.0))
            const(pool.memset(ones[:, :], 1.0))
            const(pool.memset(upper[:, :], 1.0))
            const(pool.memset(consts[:, :], EPS))
            const(pool.memset(zz[:, :, :], 0.0))
            const(pool.memset(gt[:, :, :], 0.0))
            const(pool.affine_select(out=ident, in_=ident, compare_op=ALU.not_equal, fill=1.0, base=0,
                                     pattern=[[-1, P]], channel_multiplier=1))
            const(pool.affine_select(out=upper[:, :], in_=upper[:, :], compare_op=ALU.is_ge, fill=0.0, base=0,
                                     pattern=[[1, P]], channel_multiplier=-1))
            assert steps[0] == 8
            for l in range(1, LEVELS + 1):
                m = 1 << (l - 1)
                mv = masks[:, l, :].rearrange("p (n h m) -> p n h m", h=2, m=m)
                const(pool.memset(mv[:, :, 1, :], 1.0))
                v = masks[:, l, :].rearrange("p (n w) -> p n w", w=2 * m)
                const(pool.affine_select(out=v, in_=v, compare_op=ALU.is_ge, fill=0.0, base=0,
                                         pattern=[[-2 * m, P // (2 * m)], [0, 2 * m]], channel_multiplier=1))
                const(pool.affine_select(out=v, in_=v, compare_op=ALU.is_ge, fill=0.0, base=m - 1,
                                         pattern=[[2 * m, P // (2 * m)], [0, 2 * m]], channel_multiplier=-1))
            pool.dma_start(o_gconv_s[0, :, 0:2, :], state_gdn_conv[0, :, 1:3, :]).then_inc(old_out, 16)
            pool.dma_start(o_rconv_s[0, :, 0:2, :], state_rglru_conv[0, :, 1:3, :]).then_inc(old_out, 16)
            pool.wait_ge(st_pe, 12)
            const(pool.memset(xraw[:, :, :, 0:3], 0.0))

            def history(n, slot, tile0, is_c=False):
                if not isinstance(n, int) or n > 0:
                    pool.wait_ge(conv_done, n)
                hv = params[:, C_HIST:C_HIST + 96].rearrange("p (b j k) -> p b j k", j=3, k=4) if is_c else hist_b
                wv = params[:, C_CONV:C_CONV + 16].rearrange("p (j k) -> p j k", k=4) if is_c else \
                    params[:, B_CONV:B_CONV + 96].rearrange("p (j k) -> p j k", k=24)
                for t in range(2):
                    dst = xraw[:, slot, t, 3 + L:XW].rearrange("p (b j) -> p b j", j=CONVW)
                    src = hv[:, :, :, ds(tile0 + t, 1)].rearrange("p b j o -> p b (j o)")
                    pool.tensor_copy(dst[:, :, 0:3], src).then_inc(hist_in, 1)
                    pool.tensor_copy(convw[:, slot, t, :], wv[:, :, ds(tile0 + t, 1)].rearrange("p j o -> p (j o)"))\
                        .then_inc(hist_in, 1)

            def settled():
                pool.sem_inc(passed, 1)

            def states(n, k, src):
                if not isinstance(n, int) or n > 0:
                    pool.wait_ge(mx["st"], 64 * n)
                settled()
                for j in range(2):
                    pool.dma_start(Ss[:, 8 * j:8 * j + 8, :],
                                   src[0, :, ds(2 * k + j, 1)].rearrange("b o d e -> d (b o) e")).then_inc(mx["ld"], 16)

            def store(n, k, dst_s, dst_p):
                pool.wait_ge(mx["sn"], 16 * n + 16)
                pool.wait_ge(mx["s2"], 2 * n + 2)
                settled()
                for j in range(2):
                    pool.dma_start(dst_s[0, :, ds(2 * k + j, 1)].rearrange("b o d e -> d (b o) e"),
                                   Ss[:, 8 * j:8 * j + 8, :]).then_inc(mx["st"], 16)
                    pool.dma_start(dst_p[0, 0, ds(2 * k + j, 1)].rearrange("o d e -> d (o e)"),
                                   S[:, j, 1, :]).then_inc(mx["st"], 16)

            def b_mixer(n, between=None):
                states(n, n, state_gdn)
                pool.wait_ge(mx["dec"], n + 1)
                pool.tensor_tensor(decay[:, :, :], decay[:, :, :],
                                   upper[:, :].unsqueeze(1).broadcast_to([P, 4, P]), ALU.mult).then_inc(mx["cau"], 1)
                pool.wait_ge(mx["ld"], 32 * n + 32)
                pool.wait_ge(mx["ks"], n + 1)
                pool.wait_ge(mx["pair"], 2 * n + 2)
                pool.tensor_tensor(Ss[:, :, :], Ss[:, :, :], spair[:, 0, :].unsqueeze(2).broadcast_to([P, 16, P]),
                                   ALU.mult).then_inc(mx["sdec"], 1)
                pool.wait_ge(mx["at"], 2 * n + 2)
                for l in range(2, LEVELS + 1):
                    if l == 5 and between:
                        between()
                    if l == 2:
                        pool.wait_ge(mx["tt"], n + 1)
                    else:
                        pool.wait_ge(mx["x"], 6 * n + l - 2)
                    pool.tensor_tensor(AL, AT[:, :, :], masks[:, l, :].unsqueeze(1).broadcast_to([P, 4, P]),
                                       ALU.mult).then_inc(mx["al"], 1)
                store(n, n, o_gdn_s, o_gdn_p)

            def a_mixer(n, k):
                if k:
                    pool.wait_ge(a_["vs"], k)
                states(n, k, state_hgrn)
                pool.wait_ge(mx["ld"], 32 * n + 32)
                pool.wait_ge(a_["fs"], k + 1)
                pool.tensor_tensor(Ss[:, :, :], Ss[:, :, :], small[:, 0, :].unsqueeze(2).broadcast_to([P, 16, P]),
                                   ALU.mult).then_inc(mx["sdec"], 1)
                store(n, k, o_hgrn_s, o_hgrn_p)

            const(pool.memset(wbd[:, :, :, :], 0.0))
            for w, src in enumerate((c_wa, c_wx)):
                for h in range(2):
                    pool.dma_start(wbd[64 * h:64 * h + 64, w, :, 64 * h:64 * h + 64],
                                   src[0, h:8:2].rearrange("n i j -> i n j")).then_inc(wbd_in, 16)
            pool.wait_ge(st_dve, 6)
            history(0, 0, 0)
            history(0, 1, 8)
            history(1, 0, 16)

            def b_round(r):
                history(3 * r, 0, 2 * r)
                history(3 * r, 1, 2 * r + 8)
                b_mixer(r - 1, lambda: history(3 * r + 1, 0, 2 * r + 16))

            b_round(1)
            with pool.Fori(2, B_ROUNDS) as r:
                b_round(r)
            history(12, 0, 0, is_c=True)
            history(12, 1, 2, is_c=True)
            b_mixer(3)
            a_mixer(4, 0)
            a_mixer(5, 1)
            pool.wait_ge(tl_cp, 4)
            pool.dma_start(o_gconv_p[0, 0].rearrange("j (k p) -> (j k) p", p=P), rows[0:72, 0]).then_inc(tl_out, 16)
            for b in range(NB):
                src = rows[24 * b:24 * b + 24, 1] if b < 5 else rows[24 * (b - 5):24 * (b - 5) + 24, 2]
                pool.dma_start(o_gconv_s[0, b, 2].rearrange("(k p) -> k p", p=P), src).then_inc(tl_out, 16)
            pool.dma_start(o_rconv_p[0, 0].rearrange("j (k p) -> (j k) p", p=P), rows[0:12, 3]).then_inc(tl_out, 16)
            for b in range(NB):
                pool.dma_start(o_rconv_s[0, b, 2].rearrange("(k p) -> k p", p=P),
                               rows[12 + 4 * b:16 + 4 * b, 3]).then_inc(tl_out, 16)
            pool.dma_start(o_rh_p[0, 0].rearrange("(k p) -> k p", p=P), rows[44:48, 3]).then_inc(tl_out, 16)
            pool.dma_start(o_rh_s[0].rearrange("b (k p) -> (b k) p", p=P), rows[48:80, 3]).then_inc(tl_out, 16)

            def residual_pool(n, src, dst, base):
                pool.wait_ge(o_r, 2 * n + 2)
                pool.wait_ge(drained[1], base)
                s = slice(12, 16)
                pool.tensor_tensor(src[:, s], src[:, s], rbc[:, :].unsqueeze(1).broadcast_to([P, 4, T]), ALU.mult)\
                    .then_inc(o_pool, 1)
                pool.wait_ge(o_pool, 2 * n + 1)
                pool.tensor_tensor(dst[:, s], xT[:, s], src[:, s], ALU.add).then_inc(o_pool, 1)

            residual_pool(0, mixg, xT, 18)
            residual_pool(1, ffg, ffg, 44)
            pool.wait_ge(tl_out, 16 * 20)
            pool.wait_ge(old_out, 32)
            pool.wait_ge(mx["st"], 64 * 6)

        @block.tensor
        def _(pe):
            def chunk(c, slot, par, k0, nk, x_hi, x_lo, half=None, begin=0):
                if half != 1:
                    pe.wait_ge(lo_done, c + 1)
                for m in range(2):
                    if half is not None and m != half:
                        continue
                    for k in range(CK):
                        out = ps[:, 2 * par + m, 0:T]
                        wh, wl = w_hi[:, slot, k, m * P:m * P + P], w_lo[:, slot, k, m * P:m * P + P]
                        kk = k0 + k
                        pe.matmul(out, wh, x_hi[:, kk], start=(kk == begin), stop=False)
                        pe.matmul(out, wh, x_lo[:, kk], start=False, stop=False)
                        last = pe.matmul(out, wl, x_hi[:, kk], start=False, stop=(kk == nk - 1))
                if half != 0:
                    last.then_inc(pe_used, 1)

            def bank_free(par, n):
                if not isinstance(n, int) or n > 0:
                    pe.wait_ge(drained[par], n)

            pe.wait_ge(pool_c, 8)
            pe.wait_ge(x_in, 48)
            for q in range(12):
                t, k0 = q // 4, 4 * (q % 4)
                n = P if t < 2 else NB
                if q >= 4:
                    pe.wait_ge(st_act, q - 3)
                for k in range(4):
                    last = pe.transpose(ps[:, q % 4, k * P:k * P + n],
                                        xtok[0:n, t, (k0 + k) * P:(k0 + k) * P + P], ident[0:n, 0:n])
                last.then_inc(st_pe, 1)
            pe.wait_ge(par_in, 19 * 16)
            for i, (n, bank, col) in enumerate(((112, 6, 0), (114, 6, 112), (96, 6, 226), (P, 7, 0), (P, 7, P),
                                                (P, 7, 2 * P), (P, 7, 3 * P), (64, 5, 0))):
                last = pe.transpose(ps[:, bank, col:col + n], stage[0:n, i], ident[0:n, 0:n])
            last.then_inc(st_pe, 1)

            def stats(n, bank):
                for q in range(4):
                    stats_quarter(n, bank, q)

            def stats_quarter(n, bank, q):
                pe.wait_ge(nz_sq, 4 * n + q + 1)
                for k in range(4 * q, 4 * q + 4):
                    last = pe.matmul(ps[:, bank, 0:T], ones[:, :], hF[:, k], start=(k == 0), stop=(k == KT - 1),
                                     skip_group_check=True)
                if q == 3:
                    last.then_inc(nz_pe, 1)

            stats(0, 4)
            pe.wait_ge(gw_in, 16)
            for k in range(KT):
                if k % 4 == 0:
                    pe.wait_ge(nz_h, k // 4 + 1)
                last = pe.matmul(ps[0:16, 5, 0:T], gw[:, k], hF[:, k], start=(k == 0), stop=(k == KT - 1))
            last.then_inc(st_pe, 1)
            pe.wait_ge(st_dve, 7)
            for t in range(3):
                n = P if t < 2 else NB
                last = pe.transpose(ps[0:n, 6, 16 * t:16 * t + 16], bab[0:16, t * P:t * P + n], ident[0:16, 0:16])
            last.then_inc(st_pe, 1)

            def gating():
                pe.wait_ge(st_dve, 31)
                g2 = gt[:, 0:2, 8:16]
                pe.matmul(ps[:, 6, 64:80], upper[:, :], g2, start=True, stop=True)
                pe.matmul(ps[:, 6, 80:96], ones[:, :], g2, start=True, stop=True)
                pe.matmul(ps[:, 6, 128:256], ones[0:8, :], sel[:, :, :, :], start=True, stop=True).then_inc(st_pe, 1)

            def b_step(hp, n):
                if hp == 1:
                    pe.wait_ge(mx["sq"], n + 1)
                    if not isinstance(n, int) or n > 0:
                        pe.wait_ge(mx["ors"], n)
                    for i in range(4):
                        last = pe.matmul(ps[:, 4 + i, 0:T], ones[:, :], sq[:, i], start=True, stop=True)
                    last.then_inc(mx["ss"], 1)
                if hp == 3:
                    pe.wait_ge(mx["ln"], n + 1)
                    pe.wait_ge(mx["pair"], 2 * n + 2)
                    for x in range(4):
                        pe.matmul(ps[:, 4, x * P:x * P + P], pair[:, F_G, x:x + 1].broadcast_to([P, P]), upper[:, :],
                                  start=True, stop=True)
                    for x in range(4):
                        pe.matmul(ps[:, 5, x * P:x * P + P], pair[:, F_BETA, x:x + 1].broadcast_to([P, P]), ident,
                                  start=True, stop=True)
                    for x in range(4):
                        last = pe.transpose(ps[:, 7, x * P:x * P + P],
                                            qkv[:, 2, x // 2, (x % 2) * P:(x % 2) * P + P], ident)
                    last.then_inc(mx["bc"], 1)
                if hp == 5:
                    pe.wait_ge(mx["nrm"], 2 * n + 2)
                    for x in range(4):
                        last = pe.transpose(ps[:, 6, x * P:x * P + P],
                                            nrm[:, 1, x // 2, (x % 2) * P:(x % 2) * P + P], ident)
                    last.then_inc(mx["tr"], 1)
                if hp == 6:
                    pe.wait_ge(mx["ld"], 32 * n + 32)
                    pe.wait_ge(mx["tm"], 3 * n + 3)
                    for x in range(16):
                        last = pe.matmul(ps[:, 7, 2 * x:2 * x + 2], Ss[:, x, :],
                                         nrm[:, :, x // 8, L + x % 8], start=True, stop=True)
                    last.then_inc(mx["ks"], 1)
                if hp == 7:
                    pe.wait_ge(mx["kb"], n + 1)
                    pe.wait_ge(mx["eb"], n + 1)
                    pe.wait_ge(mx["d"], 2 * n + 2)
                    for x in range(4):
                        kn = nrm[:, 1, x // 2, (x % 2) * P:(x % 2) * P + P]
                        pe.matmul(ps[:, 4, x * P:x * P + P], kn, kb[:, x, :], start=True, stop=True)
                        last = pe.matmul(ps[:, 5, x * P:x * P + P], kn,
                                         nrm[:, 0, x // 2, (x % 2) * P:(x % 2) * P + P], start=True, stop=True)
                    last.then_inc(mx["g"], 1)
                if hp == 8:
                    pe.wait_ge(mx["qkp"], n + 1)
                    pe.matmul(ps[:, 7, 32:48], ones[:, :], small[:, 0, :], start=True, stop=True).then_inc(mx["qk"], 1)
                if hp == 10:
                    pe.wait_ge(mx["tt"], n + 1)
                    for x in range(4):
                        last = pe.transpose(ps[:, 6, x * P:x * P + P], TT[:, x, :], ident)
                    last.then_inc(mx["t1"], 1)
                if 12 <= hp <= 23:
                    l = 2 + (hp - 12) // 2
                    if hp % 2 == 0:
                        pe.wait_ge(mx["al"], 6 * n + l - 1)
                        pe.wait_ge(mx["t"], 12 * n + 2 * l - 3)
                        for x in range(4):
                            last = pe.matmul(ps[:, 4, x * P:x * P + P], AL[:, x, :], TM[:, x, :], start=True, stop=True)
                        last.then_inc(mx["x"], 1)
                    else:
                        pe.wait_ge(mx["xc"], 6 * n + l - 1)
                        for x in range(4):
                            last = pe.matmul(ps[:, 5, x * P:x * P + P], XM[:, x, :], TT[:, x, :], start=True, stop=True)
                        if l < LEVELS:
                            for x in range(4):
                                last = pe.matmul(ps[:, 6, x * P:x * P + P], TT[:, x, :], XM[:, x, :],
                                                 start=True, stop=True)
                        last.then_inc(mx["p"], 1)
                if hp in (14, 16, 18, 20):
                    i = (hp - 14) // 2
                    pe.wait_ge(mx["us"], 6 * n + 5)
                    if i:
                        pe.wait_ge(mx["sn"], 16 * n + 4 * i)
                    for x in range(4):
                        last = pe.matmul(ps[:, 7, x * P:x * P + P],
                                         small[:, 3, 4 * i + x:4 * i + x + 1].broadcast_to([P, P]), ident,
                                         start=True, stop=True)
                    last.then_inc(mx["ub"], 1)
                if hp == 24:
                    pe.wait_ge(mx["t"], 12 * n + 12)
                    for j in range(2):
                        pe.matmul(ps[:, 4, j * P:j * P + P], TT[:, 2 * j, :], vb[:, 2 * j, :], start=True, stop=True)
                    for j in range(2):
                        last = pe.matmul(ps[:, 5, j * P:j * P + P], kbe[:, 2 * j + 1, :], TT[:, 2 * j + 1, :],
                                         start=True, stop=True)
                    last.then_inc(mx["u0"], 1)
                if hp == 25:
                    pe.wait_ge(mx["u0c"], 2 * n + 2)
                    for j in range(2):
                        last = pe.matmul(ps[:, 6, j * P:j * P + P], k_end[:, 2 * j, :], u[:, 2 * j, :],
                                         start=True, stop=True)
                    last.then_inc(mx["s1"], 1)
                if hp == 26:
                    pe.wait_ge(mx["s1c"], n + 1)
                    for j in range(2):
                        o = ps[:, 4, 256 + j * P:256 + j * P + P]
                        pe.matmul(o, TT[:, 2 * j + 1, :], vb[:, 2 * j + 1, :], start=True, stop=False)
                        last = pe.matmul(o, nwT[:, j, :], S[:, j, 0, :], start=False, stop=True)
                    last.then_inc(mx["u1"], 1)
                if hp == 27:
                    pe.wait_ge(mx["u1c"], n + 1)
                    for j in range(2):
                        pe.matmul(ps[:, 5, 256 + j * P:256 + j * P + P], k_end[:, 2 * j + 1, :], u[:, 2 * j + 1, :],
                                  start=True, stop=True)
                    for x in range(4):
                        o = ps[:, 6, x * P:x * P + P]
                        last = pe.matmul(o, u[:, x, :], QK[:, x, :], start=True, stop=(x % 2 == 0))
                        if x % 2:
                            last = pe.matmul(o, S[:, x // 2, 0, :], eb[:, x, :], start=False, stop=True)
                    last.then_inc(mx["so"], 1)
                if hp == 29:
                    out_sum(n)

            def out_sum(n):
                pe.wait_ge(mx["osq"], n + 1)
                pe.wait_ge(mx["s2"], 2 * n + 2)
                for j in range(2):
                    last = pe.matmul(ps[:, 4 + j, 0:T], ones[:, :], sq[:, j], start=True, stop=True)
                last.then_inc(mx["oss"], 1)

            def a_step(hp, n, k):
                if hp in (3, 5, 7, 9):
                    i = (hp - 3) // 2
                    pe.wait_ge(mx["ors"], n)
                    if i:
                        pe.wait_ge(mx["sn"], 16 * n + 4 * i)
                    for x in range(4):
                        y = 4 * i + x
                        last = pe.matmul(ps[:, 7, x * P:x * P + P],
                                         qkv[:, 2, y // 8, L + y % 8:L + y % 8 + 1].broadcast_to([P, P]), ident,
                                         start=True, stop=True)
                    last.then_inc(mx["ub"], 1)
                if hp == 12:
                    pe.wait_ge(mx["sn"], 16 * n + 16)
                    for x in range(16):
                        last = pe.matmul(ps[:, 7, x:x + 1], Ss[:, x, :], q_s[:, x:x + 1],
                                         start=True, stop=True)
                    last.then_inc(a_["vs"], 1)
                if hp == 14:
                    pe.wait_ge(a_["w"], 16 * k + 16)
                    pe.wait_ge(mx["os"], n + 1)
                    for x in range(4):
                        pe.transpose(ps[:, 6, x * P:x * P + P], kend_f[:, x, :], ident)
                    for x in range(4):
                        last = pe.transpose(ps[:, 7, x * P:x * P + P],
                                            qkv[:, 2, x // 2, (x % 2) * P:(x % 2) * P + P], ident)
                    last.then_inc(a_["tr"], 1)
                if hp in (16, 18, 20, 22):
                    x = (hp - 16) // 2
                    b0 = 4 + 2 * (x % 2)
                    if x == 1:
                        pe.wait_ge(a_["tm"], 2 * k + 2)
                    if x >= 2:
                        pe.wait_ge(a_["pr"], 8 * k + 2 * x - 2)
                    t = slice((x % 2) * P, (x % 2) * P + P)
                    pe.matmul(ps[:, b0, 0:P], nrm[:, 0, x // 2, t], qA[:, x // 2, t], start=True, stop=True)
                    for l in range(1, LEVELS + 1):
                        w = lev[:, l - 1, x * P:x * P + P]
                        last = pe.matmul(ps[:, b0 + l // 4, (l % 4) * P:(l % 4) * P + P], w, w, start=True, stop=True)
                    last.then_inc(a_["at"], 1)
                if hp == 24:
                    pe.wait_ge(a_["pr"], 8 * k + 6)
                    for j in range(2):
                        last = pe.matmul(ps[:, 4, j * P:j * P + P], ke_tm[:, 2 * j, :], v_tm[:, 2 * j, :],
                                         start=True, stop=True)
                    last.then_inc(mx["s1"], 1)
                if hp == 26:
                    pe.wait_ge(mx["s1c"], n + 1)
                    pe.wait_ge(a_["rd"], 4 * k + 4)
                    for j in range(2):
                        pe.matmul(ps[:, 5, 256 + j * P:256 + j * P + P], ke_tm[:, 2 * j + 1, :], v_tm[:, 2 * j + 1, :],
                                  start=True, stop=True)
                    for x in range(4):
                        o = ps[:, 6, x * P:x * P + P]
                        last = pe.matmul(o, v_tm[:, x, :], attT[:, x, :], start=True, stop=(x % 2 == 0))
                        if x % 2:
                            last = pe.matmul(o, S[:, x // 2, 0, :], nwT[:, x // 2, :], start=False, stop=True)
                    last.then_inc(mx["so"], 1)
                if hp == 29:
                    out_sum(n)

            def round_(r, mixer):
                for pos in range(SLOTS):
                    q = pos // 4
                    if pos % 4 == 0:
                        bank_free(q % 2, 2 * r + q // 2)
                    for half in range(2):
                        chunk(SLOTS * r + pos, pos % 4, q % 2, 4 * (pos % 4), KT, act_hi, act_lo, half)
                        mixer(2 * pos + half)

            pe.wait_ge(nz_lo, 4)
            round_(0, lambda hp: gating() if hp == 13 else None)
            round_(1, lambda hp: b_step(hp, 0))
            with pe.Fori(2, B_ROUNDS) as r:
                round_(r, lambda hp: b_step(hp, r - 1))
            round_(4, lambda hp: b_step(hp, 3))
            round_(5, lambda hp: a_step(hp, 4, 0))
            round_(6, lambda hp: a_step(hp, 5, 1))

            def gate_products(w):
                for t in range(4):
                    last = pe.matmul(ps[:, 4 + t, 0:T], wbd[:, w, t, :], qkv[:, t // 2, t % 2, :], start=True, stop=True)
                return last

            def out_stats(n, g):
                pe.wait_ge(o_sq, n + g + 1)
                for t in range(2):
                    last = pe.matmul(ps[:, 4, 0:T], ones[:, :], sqo[:, g % 2, t], start=(g == 0 and t == 0),
                                     stop=(g == 7 and t == 1), skip_group_check=True)
                last.then_inc(o_pe, 1)

            for s, (g, i) in enumerate(OUT_START):
                if i == 1:
                    bank_free(g, OUT_G0 // 2)
                if s == 4:
                    pe.wait_ge(mx["olo"], 6)
                if s == 6:
                    pe.wait_ge(c_["lo"], 1)
                chunk(OUT_C0 + s, s % RING, g, 4 * i, KT, cat_hi, cat_lo, begin=4)
                if s == 0:
                    pe.wait_ge(wbd_in, 64)
                    pe.wait_ge(silu_done, 28)
                    pe.wait_ge(mx["ors"], 6)
                    gate_products(0).then_inc(c_["r"], 1)
                if s == 1:
                    pe.wait_ge(c_["prei"], 4)
                    gate_products(1).then_inc(c_["i"], 1)
            for g in range(2, OUT_GROUPS):
                bank_free(g % 2, (OUT_G0 + g) // 2)
                for i in range(4):
                    chunk(OUT_C0 + 4 * g + i, i, g % 2, 4 * i, KT, cat_hi, cat_lo)
                    if g == 2 and i == 0:
                        out_stats(0, 0)
                    if i == 1:
                        out_stats(0, g - 1)
                    if g == 2 and i == 3:
                        pe.wait_ge(c_["h"], 5)
                        tb, tc = tail_b[:, :, :].rearrange("p a k -> p (a k)"), tail_c[:, :, :].rearrange("p a k -> p (a k)")
                        pe.transpose(ps[0:72, 6, 0:P], tb[:, 0:72], ident)
                        pe.transpose(ps[0:120, 6, P:2 * P], tb[:, 72:192], ident)
                        pe.transpose(ps[0:72, 6, 2 * P:3 * P], tb[:, 192:264], ident)
                        pe.transpose(ps[0:80, 6, 3 * P:4 * P], tc[:, 0:80], ident).then_inc(tl_pe, 1)
            out_stats(0, 7)

            for n in range(2):
                bank_free(n, FF_G0 // 2)
                for i in range(4):
                    if n == 0:
                        pe.wait_ge(nz_lo, 5 + i)
                    chunk(FF_C0 + 4 * n + i, i, n, 4 * i, KT, act_hi, act_lo)
                    if (n, i) >= (0, 2) and (n, i) <= (1, 1):
                        stats_quarter(1, 5, 4 * n + i - 2)
            with pe.Fori(1, FF_PAIRS) as g:
                for n in range(2):
                    bank_free(n, g + FF_G0 // 2)
                    for i in range(4):
                        chunk(8 * g + FF_C0 + 4 * n + i, i, n, 4 * i, KT, act_hi, act_lo)

            pe.wait_ge(nz_lo, 8 + FF_PAIRS)

            for g in range(DOWN_GROUPS):
                c0 = DOWN_CH * g
                bank_free(g % 2, (DOWN_G0 + g) // 2)
                for i in range(DOWN_CH):
                    chunk(DOWN_C0 + c0 + i, (c0 + i) % RING, g % 2, CK * i, FT, hid_hi, hid_lo)
                    if i == 1 and g:
                        out_stats(8, g - 1)
            out_stats(8, 7)

            for q in range(12):
                t, k0 = q // 4, 4 * (q % 4)
                n = P if t < 2 else NB
                if q < 3:
                    pe.wait_ge(o_y, 3 + q + 1)
                if q == 3:
                    pe.wait_ge(o_pool, 4)
                if q >= 4:
                    pe.wait_ge(y_cp, q - 3)
                for k in range(4):
                    last = pe.transpose(ps[0:n, q % 4, k * P:k * P + P], ffg[:, k0 + k, t * P:t * P + n], ident)
                last.then_inc(y_pe, 1)

        @block.scalar
        def _(act):
            def A(out, in_, f=ACT.Copy, **kw):
                return act.activation(out, in_, f, **kw)

            def split(turn, slot, first=False):
                act.wait_ge(raw_in[slot], 16 * turn + 16)
                if not first:
                    act.wait_ge(pe_used, RING * turn + slot - RING + 1)
                A(w_hi[:, slot], raw[:, slot]).then_inc(hi_done, 1)

            def ln_exp_tables():
                act.preload_act_table_set("natural_log_exp_and_others")

            for q in range(12):
                t, k0 = q // 4, 4 * (q % 4)
                n = P if t < 2 else NB
                act.wait_ge(st_pe, q + 1)
                A(xT[:, k0:k0 + 4, t * P:t * P + n], ps[:, q % 4, :].rearrange("p (k t) -> p k t", k=4)[:, :, 0:n])\
                    .then_inc(st_act, 1)
            for i in range(AHEAD):
                split(0, i, first=True)

            def rms(n):
                ln_exp_tables()
                act.wait_ge(nz_pe, n + 1)
                A(rbc[:, :], ps[:, 4 + n, 0:T], ACT.Ln, scale=1.0 / D, bias=eps).then_inc(nz_r, 1)
                act.wait_ge(nz_r, 2 * n + 1)
                A(rbc[:, :], rbc[:, :], ACT.Exp, scale=-0.5).then_inc(nz_r, 1)

            act.wait_ge(pool_c, 8)
            for q in range(4):
                act.wait_ge(st_act, 9 + q)
                A(hF[:, 4 * q:4 * q + 4], xT[:, 4 * q:4 * q + 4], ACT.Square).then_inc(nz_sq, 1)
            rms(0)
            for q in range(4):
                act.wait_ge(nz_h, q + 1)
                A(act_hi[:, 4 * q:4 * q + 4], hF[:, 4 * q:4 * q + 4]).then_inc(nz_hi, 1)

            def gating():
                act.wait_ge(st_dve, 10)
                A(zz[:, 1, :], zz[:, 0, :], ACT.Abs).then_inc(st_act, 1)
                act.wait_ge(st_act, 13)
                A(zz[:, 1, :], zz[:, 1, :], ACT.Exp, scale=-1.0).then_inc(st_act, 1)
                act.wait_ge(bc_in, 32)
                A(bcA[:, :], bcA[:, :], ACT.Exp).then_inc(st_act, 1)
                act.wait_ge(st_dve, 10)
                A(gt[:, :, 0:8], gt[:, :, 0:8], ACT.Sigmoid).then_inc(st_act, 1)
                act.wait_ge(st_pe, 16)
                A(gb[:, :, :], ps[:, 6, 64:96].rearrange("p (a b) -> p a b", a=2)).then_inc(st_act, 1)
                A(sgates[:, 0], ps[:, 6, 128:192].rearrange("p (k j) -> p k j", k=4), ACT.Exp).then_inc(st_act, 1)
                A(sgates[:, 1], ps[:, 6, 192:256].rearrange("p (k j) -> p k j", k=4)).then_inc(st_act, 1)
                act.wait_ge(st_act, 17)
                by_chunk = gb[:, :, :].rearrange("p a (c k j) -> p a c k j", c=2, k=4)
                for c in range(2):
                    gv = gates[:, :, :, c:4:2]
                    A(gv[:, F_EEND], by_chunk[:, 1, c], ACT.Exp).then_inc(st_act, 1)
                    A(gv[:, F_BETAEXP], by_chunk[:, 0, c], ACT.Exp).then_inc(st_act, 1)
                act.wait_ge(st_dve, 33)
                A(gates[:, F_KEND], gates[:, F_KEND], ACT.Exp).then_inc(st_act, 1)

            def acc_ready(g):
                act.wait_ge(pe_used, 4 * g + 4)

            def evac_conv(g, par, n, slot, tail, tile0):
                acc_ready(g)
                act.wait_ge(hist_in, 4 * n + 4)
                A(xraw[:, slot, :, 3:3 + L], acc(par)[:, :, 0:L]).then_inc(raw_q, 1)
                new = xraw[:, slot, :, 3 + L:XW].rearrange("p t (b j) -> p t b j", j=CONVW)[:, :, :, 3]
                A(new, acc(par)[:, :, L:T]).then_inc(raw_q, 1)
                A(tail[:, 0:11, ds(tile0, 2)], acc(par)[:, :, L - 3:T].rearrange("p t k -> p k t")).then_inc(drained[par], 1)

            def silu_conv(n, which, f=ACT.Silu):
                act.wait_ge(conv_done, n + 1)
                A(qkv[:, which, :, 0:L], conv[:, :, 0:L], f).then_inc(silu_done, 1)
                A(qkv[:, which, :, L:T], conv[:, :, L + 3:CW:CONVW], f).then_inc(silu_done, 1)

            def evac_plain(g, par, which, f):
                acc_ready(g)
                A(qkv[:, which], acc(par), f).then_inc(drained[par], 1)

            def b_step(pos, n):
                first = isinstance(n, int) and n == 0
                if pos == 0:
                    act.wait_ge(silu_done, 6 * n + 6)
                    if not first:
                        act.wait_ge(mx["oss"], n)
                    A(sq[:, :, :], qkv[:, 0:2].rearrange("p a j t -> p (a j) t"), ACT.Square).then_inc(mx["sq"], 1)
                if pos == 1:
                    ln_exp_tables()
                    act.wait_ge(mx["ss"], n + 1)
                    if not first:
                        act.wait_ge(mx["og"], 2 * n)
                    A(rs[:, :, :], ps[:, 4:8, 0:T], ACT.Ln, bias=eps).then_inc(mx["ln"], 1)
                    act.wait_ge(mx["ln"], n + 1)
                    A(rs[:, :, :], rs[:, :, :], ACT.Exp, scale=-0.5).then_inc(mx["rs"], 1)
                if pos == 2:
                    act.wait_ge(mx["d"], 2 * n + 1)
                    A(eb[:, :, :], quad(4), ACT.Exp).then_inc(mx["eb"], 1)
                if pos == 3:
                    act.wait_ge(mx["d"], 2 * n + 2)
                    A(decay[:, :, :], decay[:, :, :], ACT.Exp).then_inc(mx["dec"], 1)
                if pos == 5:
                    act.wait_ge(mx["t1"], n + 1)
                    A(TM, quad(6)).then_inc(mx["t"], 1)
                if 6 <= pos <= 11:
                    l = pos - 4
                    act.wait_ge(mx["x"], 6 * n + l - 1)
                    A(XM, quad(4)).then_inc(mx["xc"], 1)
                if pos == 12:
                    act.wait_ge(mx["u0"], n + 1)
                    A(u[:, 0:4:2, :], quad(4)[:, 0:2]).then_inc(mx["u0c"], 1)
                    A(nwT[:, :, :], quad(5)[:, 0:2], scale=-1.0).then_inc(mx["u0c"], 1)
                    act.wait_ge(mx["s1"], n + 1)
                    A(S[:, :, 0, :], quad(6)[:, 0:2]).then_inc(mx["s1c"], 1)
                if pos == 13:
                    act.wait_ge(mx["u1"], n + 1)
                    A(u[:, 1:4:2, :], quad(4)[:, 2:4]).then_inc(mx["u1c"], 1)
                finish(pos, n)

            def finish(pos, n):
                if pos == 13:
                    act.wait_ge(mx["so"], n + 1)
                    A(oT[:, :, 0:L], ps[:, 6, :].rearrange("p (j t) -> p j t", j=2)).then_inc(mx["oc"], 1)
                if pos == 14:
                    act.wait_ge(mx["oc"], n + 1)
                    act.wait_ge(mx["os"], n + 1)
                    A(sq[:, 0:2], oT[:, :, :], ACT.Square).then_inc(mx["osq"], 1)
                if pos == 15:
                    ln_exp_tables()
                    act.wait_ge(mx["oss"], n + 1)
                    A(rs[:, 0:2], ps[:, 4:6, 0:T], ACT.Ln, scale=1.0 / P, bias=eps).then_inc(mx["oln"], 1)
                    act.wait_ge(mx["oln"], n + 1)
                    A(rs[:, 0:2], rs[:, 0:2], ACT.Exp, scale=-0.5).then_inc(mx["ors"], 1)

            def a_step(pos, n, k):
                if pos == 0:
                    act.wait_ge(drained[1], 2 * n + 1)
                    act.wait_ge(mx["so"], n)
                    ln_exp_tables()
                    A(nrm[:, 1], qkv[:, 1], ACT.Abs).then_inc(a_["ln"], 1)
                    act.wait_ge(a_["ln"], 3 * k + 1)
                    A(nrm[:, 1], nrm[:, 1], ACT.Exp, scale=-1.0).then_inc(a_["ln"], 1)
                    act.wait_ge(a_["ln"], 3 * k + 2)
                    A(nrm[:, 1], nrm[:, 1], ACT.Ln, bias=1.0).then_inc(a_["ln"], 1)
                if pos == 1:
                    act.wait_ge(a_["lf"], 2 * k + 1)
                    A(small[:, 0, :].rearrange("p (j b) -> p j b", j=2), nrm[:, 1, :, L:T], ACT.Exp).then_inc(a_["fs"], 1)
                    act.wait_ge(a_["lf"], 2 * k + 2)
                    A(nrm[:, 0], nrm[:, 0], ACT.Exp).then_inc(a_["k"], 1)
                if pos in (3, 4):
                    h = slice(0, 4) if pos == 3 else slice(4, 7)
                    act.wait_ge(a_["d"], 14 * k + (8 if pos == 3 else 14))
                    A(lev[:, h], lev[:, h], ACT.Exp).then_inc(a_["e"], 1)
                if pos == 2:
                    act.wait_ge(a_["b"], 4 * k + 4)
                    for x in range(4):
                        A(kend_f[:, x, :], bA[:, x, :], ACT.Exp, scale=-1.0, bias=bA[:, x, P - 1:P]).then_inc(a_["ex"], 1)
                    A(nwT[:, :, :], bA[:, 1:4:2, :], ACT.Exp).then_inc(a_["ex"], 1)
                    A(small[:, 1, 0:4], bA[:, :, P - 1], ACT.Exp).then_inc(a_["ex"], 1)
                if pos == 7:
                    act.wait_ge(a_["tr"], k + 1)
                    A(ke_tm, quad(6)).then_inc(a_["tm"], 1)
                    A(v_tm, quad(7)).then_inc(a_["tm"], 1)
                if pos == 12:
                    act.wait_ge(mx["s1"], n + 1)
                    A(S[:, :, 0, :], quad(4)[:, 0:2]).then_inc(mx["s1c"], 1)
                finish(pos, n)

            def round_(r, kind, prev, mixer):
                for pos in range(SLOTS):
                    slot, turn = (pos + AHEAD) % RING, (pos + AHEAD) // RING
                    split(4 * r + turn, slot, first=(isinstance(r, int) and r == 0 and pos + AHEAD < RING))
                    q = pos // 4
                    if pos in (4, 8, 12):
                        evac_group(r, kind, q - 1)
                    if prev and pos == 6:
                        act.wait_ge(drained[1], 2 * r)
                        A(qkv[:, 3], qkv[:, 3], ACT.Silu).then_inc(g_done, 1)
                    if kind == "a" and pos == 6:
                        act.wait_ge(drained[0], 2 * r + 1)
                        A(qkv[:, 0], qkv[:, 0], ACT.Silu).then_inc(g_done, 1)
                    if kind == "b" and pos in (6, 10, 14):
                        if not isinstance(r, int) or r > 0:
                            act.wait_ge(mx["nrm"], 2 * r)
                            if pos == 14:
                                act.wait_ge(mx["us"], 6 * r)
                        silu_conv(3 * r + q - 1, q - 1)
                    if kind == "c" and pos in (6, 10):
                        free_qkv(r, q - 1)
                        silu_conv(12 + q - 1, q - 1, ACT.Copy)
                    mixer(pos)
                    if prev and pos == 1:
                        if not isinstance(r, int) or r > 1:
                            act.wait_ge(mx["og"], 2 * r - 2)
                        evac_plain(4 * r - 1, 1, 3, ACT.Copy)

            def evac_group(r, kind, q):
                if kind == "b":
                    evac_conv(4 * r + q, q % 2, 3 * r + q, q % 2, tail_b, 2 * r + 8 * q)
                elif kind == "a":
                    free_qkv(r, q)
                    evac_plain(4 * r + q, q % 2, q, ACT.Copy)
                elif q < 2:
                    evac_conv(4 * r + q, q % 2, 12 + q, q % 2, tail_c, 2 * q)
                else:
                    free_qkv(r, q)
                    evac_plain(4 * r + q, q % 2, q, ACT.Gelu_apprx_tanh)

            def free_qkv(r, q):
                n = r - 1
                if n < B_ROUNDS:
                    act.wait_ge(mx["nrm"], 2 * n + 2)
                    if q == 2:
                        act.wait_ge(mx["us"], 6 * n + 6)
                elif q == 0:
                    act.wait_ge(a_["q"], 2 * (n - B_ROUNDS) + 2)
                elif q == 1:
                    act.wait_ge(a_["lf"], 2 * (n - B_ROUNDS) + 2)
                else:
                    act.wait_ge(a_["tr"], n - B_ROUNDS + 1)

            def mixer0(pos):
                if pos == 5:
                    gating()

            round_(0, "b", False, mixer0)
            round_(1, "b", True, lambda pos: b_step(pos, 0))
            with act.Fori(2, B_ROUNDS) as r:
                round_(r, "b", True, lambda pos: b_step(pos, r - 1))
            round_(4, "a", True, lambda pos: b_step(pos, 3))
            round_(5, "a", True, lambda pos: a_step(pos, 4, 0))
            round_(6, "c", True, lambda pos: a_step(pos, 5, 1))

            def out_evac(g, par, n, k, c_ready, gain, dst):
                act.wait_ge(pe_used, c_ready)
                if k >= 2:
                    act.wait_ge(o_pe, n + k - 1)
                if n == 0 and k == 0:
                    act.wait_ge(mx["st"], 64 * (ROUNDS - 1))
                A(sqo[:, k % 2], acc(par), ACT.Square).then_inc(o_sq, 1)
                for t in range(2):
                    tile = 2 * k + t
                    last = A(dst[:, tile], ps[:, 2 * par + t, 0:T], scale=params[:, gain + tile:gain + tile + 1])
                    if t == 1:
                        last.then_inc(drained[par], 1)

            def rg_step(pos):
                if pos == 0:
                    act.wait_ge(mx["og"], 12)
                    evac_plain(27, 1, 3, ACT.Gelu_apprx_tanh)
                if pos == 1:
                    act.wait_ge(c_["r"], 1)
                    for t in range(4):
                        A(nrm[:, t // 2, t % 2], ps[:, 4 + t, 0:T], ACT.Sigmoid,
                          bias=params[:, C_BA + t:C_BA + t + 1]).then_inc(c_["prei"], 1)
                if pos == 2:
                    act.wait_ge(c_["i"], 1)
                    for t in range(4):
                        A(rs[:, t], ps[:, 4 + t, 0:T], ACT.Sigmoid,
                          bias=params[:, C_BX + t:C_BX + t + 1]).then_inc(c_["prei"], 1)
                    act.wait_ge(c_["prei"], 4)
                    act.wait_ge(st_dve, 34)
                    for t in range(4):
                        A(ca[:, t], nrm[:, t // 2, t % 2], ACT.Exp, scale=lamc[:, 0, t:t + 1]).then_inc(c_["a"], 1)
                    for t in range(4):
                        A(cth[:, t], nrm[:, t // 2, t % 2], ACT.Tanh, scale=lamc[:, 1, t:t + 1]).then_inc(c_["a"], 1)
                if pos == 4:
                    act.wait_ge(c_["x"], 2)
                    A(cm[:, :, :], cm[:, :, :], ACT.Sqrt).then_inc(c_["a"], 1)

            for pos in range(4 * OUT_GROUPS):
                slot = (pos + AHEAD) % RING
                split((OUT_C0 + pos + AHEAD) // RING, slot)
                rg_step(pos)
                if pos == 7:
                    out_evac(0, 0, 0, 0, OUT_C0 + 7, G_MIX_POST, mixg)
                elif pos > 7 and pos % 4 == 0:
                    g = pos // 4 - 1
                    out_evac(g, g % 2, 0, g, OUT_C0 + 4 * g + 4, G_MIX_POST, mixg)
            g = OUT_GROUPS - 1
            out_evac(g, g % 2, 0, g, OUT_C0 + 4 * g + 4, G_MIX_POST, mixg)

            def out_norm(n, bank):
                act.wait_ge(o_pe, 8 * n + 8)
                if n == 0:
                    act.wait_ge(nz_lo, 4)
                ln_exp_tables()
                A(rbc[:, :], ps[:, bank, 0:T], ACT.Ln, scale=1.0 / D, bias=eps).then_inc(o_r, 1)
                act.wait_ge(o_r, 2 * n + 1)
                A(rbc[:, :], rbc[:, :], ACT.Exp, scale=-0.5).then_inc(o_r, 1)

            out_norm(0, 4)
            for q in range(4):
                if q < 3:
                    act.wait_ge(o_y, q + 1)
                else:
                    act.wait_ge(o_pool, 2)
                for k in range(4 * q, 4 * q + 4):
                    last = A(act_hi[:, k], xT[:, k], scale=params[:, G_FFN_PRE + k:G_FFN_PRE + k + 1])
                last.then_inc(nz_hi, 1)

            def gate_silu(g):
                act.wait_ge(drained[0], g + FF_G0 // 2 + 1)
                A(sgate[:, :, :], sgate[:, :, :], ACT.Silu).then_inc(gate_act, 1)

            def hid_split(g):
                act.wait_ge(drained[1], g + FF_G0 // 2 + 1)
                act.wait_ge(tl_out, 16 * 20)
                A(hid_hi[:, ds(2 * g, 2)], hidF[:, :, :]).then_inc(ff_hi, 1)

            for i in range(8):
                slot, turn = (i + AHEAD) % RING, (i + AHEAD) // RING
                split(FF_C0 // RING + turn, slot)
                if i < 4:
                    A(hF[:, 4 * i:4 * i + 4], xT[:, 4 * i:4 * i + 4], ACT.Square).then_inc(nz_sq, 1)
                if i == 5:
                    act.wait_ge(o_y, 3)
                    act.wait_ge(o_pool, 2)
                    rms(1)
                if i == 7:
                    gate_silu(0)
            with act.Fori(1, FF_PAIRS) as g:
                for i in range(8):
                    slot, turn = (i + AHEAD) % RING, (i + AHEAD) // RING
                    split(2 * g + FF_C0 // RING + turn, slot)
                    if i == 1:
                        hid_split(g - 1)
                    if i == 5:
                        gate_silu(g)
            hid_split(FF_PAIRS - 1)
            for g in range(DOWN_GROUPS):
                for i in range(DOWN_CH):
                    c = DOWN_CH * g + i + AHEAD
                    if DOWN_C0 + c < CHUNKS:
                        split((DOWN_C0 + c) // RING, c % RING)
                    if i == 0 and g:
                        out_evac(g - 1, (g - 1) % 2, 8, g - 1, DOWN_C0 + DOWN_CH * g, G_FFN_POST, ffg)
            g = DOWN_GROUPS
            out_evac(g - 1, (g - 1) % 2, 8, g - 1, DOWN_C0 + DOWN_CH * g, G_FFN_POST, ffg)
            out_norm(1, 4)
            for q in range(0, 12):
                t, k0 = q // 4, 4 * (q % 4)
                n = P if t < 2 else NB
                act.wait_ge(y_pe, q + 1)
                A(ytok[0:n, t, k0 * P:k0 * P + 512], ps[0:n, q % 4, :]).then_inc(y_cp, 1)

        @block.vector
        def _(dve):
            mul, add, sub = ALU.mult, ALU.add, ALU.subtract
            tt, stt, tsc = dve.tensor_tensor, dve.scalar_tensor_tensor, dve.tensor_scalar

            def lo(c, slot):
                dve.wait_ge(hi_done, c + 1)
                tt(w_lo[:, slot], raw[:, slot], w_hi[:, slot].bitcast(F32), sub).then_inc(lo_done, 1)

            def normalise():
                dve.wait_ge(nz_r, 2)
                for q in range(4):
                    for k in range(4 * q, 4 * q + 4):
                        g = params[:, G_MIX_PRE + k:G_MIX_PRE + k + 1]
                        last = stt(hF[:, k], xT[:, k], g, rbc[:, :], mul, mul)
                    last.then_inc(nz_h, 1)
                for q in range(4):
                    dve.wait_ge(nz_hi, q + 1)
                    s = slice(4 * q, 4 * q + 4)
                    tt(act_lo[:, s], hF[:, s], act_hi[:, s].bitcast(F32), sub).then_inc(nz_lo, 1)

            dve.wait_ge(st_pe, 13)
            dve.tensor_copy(params[:, :], ps[:, 6, 0:PCOLS]).then_inc(st_dve, 1)
            hv = hist_b[:, :, :, :].rearrange("p b j k -> p (b j k)")
            dve.tensor_copy(hv[:, 0:512], ps[:, 7, :]).then_inc(st_dve, 1)
            dve.tensor_copy(hv[:, 512:576], ps[:, 5, 0:64]).then_inc(st_dve, 1)
            for i in range(3):
                dve.memset(small[:, i, :], 0.0).then_inc(st_dve, 1)
            dve.wait_ge(st_dve, 3)
            for i in range(AHEAD):
                lo(i, i)
            normalise()
            dve.wait_ge(st_pe, 14)
            dve.tensor_copy(bab[:, :], ps[0:16, 5, 0:T]).then_inc(st_dve, 1)

            def gating():
                dve.wait_ge(st_pe, 15)
                dve.wait_ge(pool_c, 8)
                dve.tensor_copy(gt[:, 0:2, :], ps[:, 6, 0:32].rearrange("p (a b) -> p a b", a=2)).then_inc(st_dve, 1)
                dve.tensor_copy(gt[0:NB, 2, :], ps[0:NB, 6, 32:48]).then_inc(st_dve, 1)
                dve.wait_ge(st_dve, 9)
                dve.wait_ge(bc_in, 32)
                z = zz[:, 0, 0:24].rearrange("p (a b) -> p a b", a=3)
                tt(z, gt[:, :, 8:16], bcD[:, :].unsqueeze(1).broadcast_to([P, 3, 8]), add)
                tsc(zz[:, 0, 24:28], params[:, C_LAM:C_LAM + 4], -1.0, None, mul).then_inc(st_dve, 1)
                dve.wait_ge(st_act, 14)
                n = [10]

                def link(ins):
                    ins.then_inc(st_dve, 1)
                    n[0] += 1
                    dve.wait_ge(st_dve, n[0])

                link(tsc(zz[:, 2, :], zz[:, 1, :], 2.0, None, add))
                link(dve.reciprocal(zz[:, 2, :], zz[:, 2, :]))
                link(tt(zz[:, 2, :], zz[:, 2, :], zz[:, 1, :], mul))
                link(tt(zz[:, 3, :], zz[:, 2, :], zz[:, 2, :], mul))
                link(tsc(zz[:, 4, :], zz[:, 3, :], SERIES[0], None, mul))
                for c in SERIES[1:-1]:
                    link(stt(zz[:, 4, :], zz[:, 4, :], c, zz[:, 3, :], add, mul))
                link(stt(zz[:, 4, :], zz[:, 4, :], 1.0, zz[:, 2, :], add, mul))
                link(tsc(zz[:, 5, :], zz[:, 0, :], 0.0, None, ALU.max))
                link(stt(zz[:, 4, :], zz[:, 4, :], 2.0, zz[:, 5, :], mul, add))
                link(tsc(lamc[:, 1, :], zz[:, 4, 24:28], 8.0, None, mul))
                link(tsc(lamc[:, 0, :], zz[:, 4, 24:28], -8.0, None, mul))
                dve.wait_ge(st_act, 16)
                sp_ = zz[:, 4, 0:24].rearrange("p (a b) -> p a b", a=3)
                link(stt(gt[:, :, 8:16], sp_, -1.0, bcA[:, :].unsqueeze(1).broadcast_to([P, 3, 8]), mul, mul))
                for i, c0 in enumerate((8, 0)):
                    link(tt(sel[:, i], gt[0:8, 2, c0:c0 + 8].unsqueeze(2).broadcast_to([8, 8, 8]),
                            ident[0:8, 0:8].unsqueeze(1).broadcast_to([8, 8, 8]), mul))
                assert n[0] == 28 + 1, n[0]
                gtv = gt[:, 0:2, :].rearrange("p c (f k j) -> p c f k j", f=2, k=4)
                for c in range(2):
                    gv = gates[:, :, :, c:4:2]
                    dve.tensor_copy(gv[:, F_BETA], gtv[:, c, 0])
                    link(dve.tensor_copy(gv[:, F_G], gtv[:, c, 1]))
                dve.wait_ge(st_act, 23)
                gbv = gb[:, :, :].rearrange("p a (c k j) -> p a c k j", c=2, k=4)
                for c in range(2):
                    gv = gates[:, :, :, c:4:2]
                    dve.tensor_copy(gv[:, F_B], gbv[:, 0, c])
                    link(tt(gv[:, F_KEND], gbv[:, 1, c], gbv[:, 0, c], sub))
                tt(gates[:, F_BETAEXP], gates[:, F_BETAEXP], gates[:, F_BETA], mul).then_inc(st_dve, 1)

            chain = sem("dve_chain")
            chained = [0]

            def link(ins, base=0):
                ins.then_inc(chain, 1)
                chained[0] += 1
                dve.wait_ge(chain, base + chained[0])

            def after(s, n):
                if not isinstance(n, int) or n > 0:
                    dve.wait_ge(s, n)

            def convolve(n, slot, base, bias=None):
                dve.wait_ge(raw_q, 2 * n + 2)
                after(silu_done, 2 * n)
                for j in range(CONVW):
                    for t in range(2):
                        w = convw[:, slot, t, j:j + 1]
                        x = xraw[:, slot, t, j:j + CW]
                        if j == 0 and bias is not None:
                            ins = tsc(conv[:, t], x, w, bias[:, t:t + 1], mul, add)
                        elif j == 0:
                            ins = tsc(conv[:, t], x, w, None, mul)
                        else:
                            ins = stt(conv[:, t], x, w, conv[:, t], mul, add)
                    if j < CONVW - 1:
                        link(ins, base)
                    else:
                        ins.then_inc(conv_done, 1)

            def b_step(pos, n):
                up4 = lambda f: pair[:, f, :].unsqueeze(2).broadcast_to([P, 4, P])
                if pos == 0:
                    after(mx["so"], n)
                    dve.tensor_copy(pair[:, :, :], gates[:, :, ds(n, 1), :].rearrange("p f o x -> p f (o x)"))\
                        .then_inc(mx["pair"], 1)
                    dve.tensor_copy(spair[:, :, :], sgates[:, :, ds(n, 1), :].rearrange("p f o x -> p f (o x)"))\
                        .then_inc(mx["pair"], 1)
                if pos == 1:
                    dve.wait_ge(mx["rs"], n + 1)
                    rv = rs[:, :, :].rearrange("p (a j) t -> p a j t", a=2)
                    stt(nrm[:, 0], qkv[:, 0], float(P) ** -0.5, rv[:, 0], mul, mul).then_inc(mx["nrm"], 1)
                    tt(nrm[:, 1], qkv[:, 1], rv[:, 1], mul).then_inc(mx["nrm"], 1)
                if pos == 2:
                    dve.wait_ge(mx["bc"], n + 1)
                    dve.wait_ge(mx["pair"], 2 * n + 2)
                    dve.wait_ge(mx["nrm"], 2 * n + 2)
                    tt(decay[:, :, :], quad(4), up4(F_B), sub).then_inc(mx["d"], 1)
                    dve.wait_ge(mx["d"], 2 * n + 1)
                    tsc(decay[:, :, :], decay[:, :, :], 0.0, None, ALU.min).then_inc(mx["d"], 1)
                    kn = nrm[:, 1, :, 0:L]
                    tt(kb[:, :, :].rearrange("p (j c) t -> p j (c t)", j=2), kn,
                       ps[:, 5, :].rearrange("p (j t) -> p j t", j=2), mul).then_inc(mx["kb"], 1)
                    tt(vb[:, :, :], quad(7), up4(F_BETA), mul).then_inc(mx["tm"], 1)
                    dve.wait_ge(mx["tr"], n + 1)
                    tt(k_end[:, :, :], quad(6), up4(F_KEND), mul).then_inc(mx["tm"], 1)
                    tt(kbe[:, :, :], quad(6), up4(F_BETAEXP), mul).then_inc(mx["tm"], 1)
                if pos == 3:
                    dve.wait_ge(mx["eb"], n + 1)
                    tt(eb[:, :, :].rearrange("p (j c) t -> p j (c t)", j=2), nrm[:, 0, :, 0:L],
                       eb[:, :, :].rearrange("p (j c) t -> p j (c t)", j=2), mul).then_inc(mx["qe"], 1)
                    tt(small[:, 0, :].rearrange("p (j b) -> p j b", j=2), nrm[:, 0, :, L:T], nrm[:, 1, :, L:T], mul)\
                        .then_inc(mx["qkp"], 1)
                if pos == 4:
                    dve.wait_ge(mx["g"], n + 1)
                    dve.wait_ge(mx["cau"], n + 1)
                    tt(AT[:, :, :], quad(4), decay[:, :, :], mul).then_inc(mx["at"], 1)
                    dve.wait_ge(mx["at"], 2 * n + 1)
                    m1 = masks[:, 1, :].unsqueeze(1).broadcast_to([P, 4, P])
                    tt(AL, AT[:, :, :], m1, mul).then_inc(mx["qe"], 1)
                    dve.wait_ge(mx["qe"], 2 * n + 2)
                    tt(TT[:, :, :], ident.unsqueeze(1).broadcast_to([P, 4, P]), AL, sub).then_inc(mx["tt"], 1)
                    tt(QK[:, :, :], quad(5), decay[:, :, :], mul).then_inc(mx["at"], 1)
                if pos == 5:
                    dve.wait_ge(mx["ks"], n + 1)
                    dve.wait_ge(mx["qk"], n + 1)
                    kq = ps[:, 7, 0:32].rearrange("p (x two) -> p x two", two=2)
                    n5 = 6 * n
                    tt(small[:, 2, :], kq[:, :, 1], spair[:, 0, :], mul).then_inc(mx["us"], 1)
                    tt(small[:, 4, :], kq[:, :, 0], spair[:, 0, :], mul).then_inc(mx["us"], 1)
                    dve.tensor_copy(small[:, 5, :], ps[:, 7, 32:48]).then_inc(mx["us"], 1)
                    dve.wait_ge(mx["us"], n5 + 1)
                    v_s = qkv[:, 2, :, L:T]
                    j2 = lambda a: a.rearrange("p (j b) -> p j b", j=2)
                    tt(j2(small[:, 2, :]), v_s, j2(small[:, 2, :]), sub).then_inc(mx["us"], 1)
                    dve.wait_ge(mx["us"], n5 + 4)
                    tt(small[:, 3, :], small[:, 2, :], spair[:, 1, :], mul).then_inc(mx["us"], 1)
                    dve.wait_ge(mx["us"], n5 + 5)
                    tt(small[:, 5, :], small[:, 5, :], small[:, 3, :], mul).then_inc(mx["us"], 1)
                    dve.wait_ge(mx["us"], n5 + 6)
                    tt(oT[:, :, L:T], j2(small[:, 4, :]), j2(small[:, 5, :]), add).then_inc(mx["os"], 1)
                if 6 <= pos <= 11:
                    l = pos - 4
                    dve.wait_ge(mx["p"], 6 * n + l - 1)
                    if l < LEVELS:
                        tt(TM, TM, quad(6), sub).then_inc(mx["t"], 1)
                    tt(TT[:, :, :], TT[:, :, :], quad(5), sub).then_inc(mx["t"], 1)
                if 7 <= pos <= 10:
                    state_update(n, pos - 7, nrm[:, 1])
                if pos == 13:
                    dve.wait_ge(mx["so"], n + 1)
                    dve.wait_ge(mx["s1c"], n + 1)
                    after(mx["st"], 64 * n)
                    for j in range(2):
                        stt(S[:, j, 1, :], S[:, j, 0, :], pair[:, F_EEND, 2 * j + 1:2 * j + 2],
                            quad(5)[:, 2 + j], mul, add).then_inc(mx["s2"], 1)

            def state_update(n, i, k_f):
                if i == 0:
                    dve.wait_ge(mx["sdec"], n + 1)
                dve.wait_ge(mx["ub"], 4 * n + i + 1)
                for x in range(4 * i, 4 * i + 4):
                    stt(Ss[:, x, :], ps[:, 7, (x % 4) * P:(x % 4) * P + P],
                        k_f[:, x // 8, L + x % 8:L + x % 8 + 1], Ss[:, x, :], mul, add).then_inc(mx["sn"], 1)

            def finish(n, tile0, gain):
                dve.wait_ge(mx["ors"], n + 1)
                stt(oT[:, :, :], oT[:, :, :], params[:, gain:gain + 1], rs[:, 0:2], mul, mul).then_inc(mx["og"], 1)
                dve.wait_ge(mx["og"], 2 * n + 1)
                tt(oT[:, :, :], oT[:, :, :], qkv[:, 3], mul).then_inc(mx["og"], 1)
                dve.wait_ge(mx["og"], 2 * n + 2)
                dve.tensor_copy(cat_hi[:, ds(tile0, 2)], oT[:, :, :]).then_inc(mx["ohi"], 1)
                dve.wait_ge(mx["ohi"], n + 1)
                tt(cat_lo[:, ds(tile0, 2)], oT[:, :, :], cat_hi[:, ds(tile0, 2)].bitcast(F32), sub)\
                    .then_inc(mx["olo"], 1)

            def a_step(pos, n, k):
                if pos == 0:
                    dve.wait_ge(mx["so"], n)
                    dve.wait_ge(a_["ln"], 3 * k + 3)
                    dve.tensor_copy(qA, qkv[:, 0, :, 0:L]).then_inc(a_["q"], 1)
                    dve.tensor_copy(q_s.rearrange("p (j b) -> p j b", j=2), qkv[:, 0, :, L:T]).then_inc(a_["q"], 1)
                    stt(nrm[:, 1], qkv[:, 1], 0.0, nrm[:, 1], ALU.min, sub).then_inc(a_["lf"], 1)
                    dve.wait_ge(a_["lf"], 2 * k + 1)
                    tt(nrm[:, 0], nrm[:, 1], qkv[:, 1], sub).then_inc(a_["lf"], 1)
                    for x in range(4):
                        dve.tensor_tensor_scan(bA[:, x, :], ones[:, :], nrm[:, 1, x // 2, (x % 2) * P:(x % 2) * P + P],
                                               0.0, mul, add).then_inc(a_["b"], 1)
                if pos in (1, 2):
                    dve.wait_ge(a_["b"], 4 * k + 4)
                    for l in (range(0, 4) if pos == 1 else range(4, LEVELS)):
                        m = 1 << l
                        v = lambda a: a.rearrange("p (n h m) -> p n h m", h=2, m=m)
                        bv = v(sqv[:, 0:512])
                        mid = bv[:, :, 0, m - 1:m].broadcast_to([P, 256 // m, m])
                        tt(v(lev[:, l])[:, :, 0], mid, bv[:, :, 0], sub).then_inc(a_["d"], 1)
                        tt(v(lev[:, l])[:, :, 1], bv[:, :, 1], mid, sub).then_inc(a_["d"], 1)
                if pos in (2, 3, 4, 5):
                    dve.wait_ge(a_["k"], k + 1)
                    state_update(n, pos - 2, nrm[:, 0])
                if pos == 3:
                    dve.wait_ge(a_["ex"], 6 * k + 6)
                    j2 = lambda a: a.rearrange("p (j c) t -> p j (c t)", j=2)
                    tt(j2(kend_f), j2(kend_f), nrm[:, 0, :, 0:L], mul).then_inc(a_["w"], 1)
                    dve.wait_ge(a_["q"], 2 * k + 2)
                    tt(nwT[:, :, :], nwT[:, :, :], qA[:, :, P:L], mul).then_inc(a_["w"], 1)
                if pos in (4, 5):
                    dve.wait_ge(a_["e"], 2 * k + pos - 3)
                    for l in (range(0, 4) if pos == 4 else range(4, 7)):
                        m = 1 << l
                        h = lambda a: a.rearrange("p (n h m) -> p n h m", h=2, m=m)
                        for half, src in ((0, nrm[:, 0]), (1, qA)):
                            for_j = lev[:, l].rearrange("p (j n h m) -> p j n h m", j=2, h=2, m=m)[:, :, :, half]
                            sv = src[:, :, 0:L].rearrange("p j (n h m) -> p j n h m", h=2, m=m)[:, :, :, half]
                            tt(for_j, for_j, sv, mul).then_inc(a_["w"], 1)
                if pos == 6:
                    dve.wait_ge(a_["vs"], k + 1)
                    dve.tensor_copy(oT[:, :, L:T], ps[:, 7, 0:16].rearrange("p (j b) -> p j b", j=2))\
                        .then_inc(mx["os"], 1)
                if pos in (8, 9, 10, 11):
                    x = pos - 8
                    b0 = 4 + 2 * (x % 2)
                    dve.wait_ge(a_["at"], 4 * k + x + 1)
                    if x:
                        dve.wait_ge(a_["rd"], 4 * k + x)
                    for h in range(2):
                        tt(prod[:, 4 * h:4 * h + 4], quad(b0 + h), masks[:, 4 * h:4 * h + 4, :], mul)\
                            .then_inc(a_["pr"], 1)
                    dve.wait_ge(a_["pr"], 8 * k + 2 * x + 2)
                    dve.tensor_reduce(attT[:, x, :], prod.rearrange("p l t -> p t l"), AX.X, ALU.add)\
                        .then_inc(a_["rd"], 1)
                if pos == 13:
                    dve.wait_ge(mx["so"], n + 1)
                    dve.wait_ge(mx["st"], 64 * n)
                    for j in range(2):
                        stt(S[:, j, 1, :], S[:, j, 0, :], small[:, 1, 2 * j + 1:2 * j + 2], quad(5)[:, 2 + j],
                            mul, add).then_inc(mx["s2"], 1)

            CV = 3

            def round_(r, kind, mixer, fin):
                for pos in range(SLOTS):
                    lo(SLOTS * r + pos + AHEAD, (pos + AHEAD) % RING)
                    q = pos // 4
                    if kind == "b" and pos in (4, 8, 12):
                        chained[0] = CV * (q - 1)
                        convolve(3 * r + q - 1, (q - 1) % 2, 3 * CV * r)
                    if kind == "c" and pos in (4, 8):
                        chained[0] = CV * (q - 1)
                        convolve(12 + q - 1, (q - 1) % 2, 12 * CV, params[:, C_BIAS + 2 * (q - 1):C_BIAS + 2 * q])
                    mixer(pos)
                    if pos == 15 and fin is not None:
                        finish(*fin)

            def mixer0(pos):
                if pos == 5:
                    gating()

            round_(0, "b", mixer0, None)
            dve.wait_ge(st_act, 24)
            dve.wait_ge(st_dve, 34)
            round_(1, "b", lambda pos: b_step(pos, 0), (0, 4, B_NORM))
            with dve.Fori(2, B_ROUNDS) as r:
                round_(r, "b", lambda pos: b_step(pos, r - 1), (r - 1, 2 * r + 2, B_NORM))
            round_(4, "a", lambda pos: b_step(pos, 3), (3, 10, B_NORM))
            round_(5, "a", lambda pos: a_step(pos, 4, 0), (4, 0, A_NORM))
            round_(6, "c", lambda pos: a_step(pos, 5, 1), (5, 2, A_NORM))

            def rg_step(pos):
                if pos == 2:
                    dve.wait_ge(c_["a"], 8)
                    tt(cm[:, :, :], ca[:, :, :], ca[:, :, :], mul).then_inc(c_["x"], 1)
                    dve.wait_ge(c_["x"], 1)
                    stt(cm[:, :, :], cm[:, :, :], 1.0, cth[:, :, :], add, mul).then_inc(c_["x"], 1)
                if pos == 3:
                    dve.wait_ge(c_["prei"], 8)
                    xc = qkv[:, 0:2].rearrange("p a j t -> p (a j) t")
                    tt(rs[:, :, :], rs[:, :, :], xc, mul).then_inc(c_["x"], 1)
                if pos == 4:
                    dve.wait_ge(c_["a"], 9)
                    dve.memset(cm[:, :, 0:1], 1.0).then_inc(c_["x"], 1)
                    dve.wait_ge(c_["x"], 4)
                    tt(cm[:, :, :], cm[:, :, :], rs[:, :, :], mul).then_inc(c_["x"], 1)
                    dve.wait_ge(c_["x"], 5)
                    for t in range(4):
                        last = dve.tensor_tensor_scan(sq[:, t, 0:L], ca[:, t, 0:L], cm[:, t, 0:L], 0.0, mul, add)
                    last.then_inc(c_["h"], 1)
                    h0 = params[:, RG_H:RG_H + 32].rearrange("p (b k) -> p k b", k=4)
                    tt(sq[:, :, L:T], ca[:, :, L:T], h0, mul).then_inc(c_["h"], 1)
                    dve.wait_ge(c_["h"], 2)
                    tt(sq[:, :, L:T], sq[:, :, L:T], cm[:, :, L:T], add).then_inc(c_["h"], 1)
                    dve.wait_ge(c_["h"], 3)
                    dve.wait_ge(drained[1], 14)
                    tt(cm[:, :, :], sq[:, :, :], qkv[:, 2:4].rearrange("p a j t -> p (a j) t"), mul).then_inc(c_["h"], 1)
                    dve.wait_ge(c_["h"], 4)
                    dve.tensor_copy(cat_hi[:, 12:16], cm[:, :, :]).then_inc(c_["hi"], 1)
                    dve.wait_ge(c_["hi"], 1)
                    tt(cat_lo[:, 12:16], cm[:, :, :], cat_hi[:, 12:16].bitcast(F32), sub).then_inc(c_["lo"], 1)
                if pos == 6:
                    dve.tensor_copy(tail_c[:, 11:20, :], sq[:, :, L - 1:T].rearrange("p k t -> p t k")).then_inc(c_["h"], 1)

            for pos in range(4 * OUT_GROUPS):
                lo(OUT_C0 + pos + AHEAD, (pos + AHEAD) % RING)
                rg_step(pos)
                if pos == 13:
                    dve.wait_ge(tl_pe, 1)
                    for i, n in enumerate((72, 120, 72, 80)):
                        dve.tensor_copy(rows[0:n, i, :], ps[0:n, 6, i * P:i * P + P]).then_inc(tl_cp, 1)

            def scale_quarter(n, q, src):
                s = slice(4 * q, 4 * q + 4)
                tt(src[:, s], src[:, s], rbc[:, :].unsqueeze(1).broadcast_to([P, 4, T]), mul).then_inc(o_g, 1)

            def add_quarter(n, q, src, dst):
                dve.wait_ge(o_g, 3 * n + q + 1)
                s = slice(4 * q, 4 * q + 4)
                tt(dst[:, s], xT[:, s], src[:, s], add).then_inc(o_y, 1)

            def input_lo(q):
                dve.wait_ge(nz_hi, 5 + q)
                for k in range(4 * q, 4 * q + 4):
                    last = stt(act_lo[:, k], xT[:, k], params[:, G_FFN_PRE + k:G_FFN_PRE + k + 1],
                               act_hi[:, k].bitcast(F32), mul, sub)
                last.then_inc(nz_lo, 1)

            dve.wait_ge(o_r, 2)
            dve.wait_ge(drained[1], 18)
            scale_quarter(0, 0, mixg)
            add_quarter(0, 0, mixg, xT)
            scale_quarter(0, 1, mixg)
            input_lo(0)
            add_quarter(0, 1, mixg, xT)
            scale_quarter(0, 2, mixg)
            input_lo(1)
            add_quarter(0, 2, mixg, xT)
            input_lo(2)

            def gate_scale(g):
                dve.wait_ge(pe_used, 8 * g + FF_C0 + 4)
                if not isinstance(g, int) or g > 0:
                    dve.wait_ge(drained[1], g + FF_G0 // 2)
                tt(sgate[:, :, :], acc(0), rbc[:, :].unsqueeze(1).broadcast_to([P, 2, T]), mul).then_inc(drained[0], 1)

            def gate_times_r(g):
                dve.wait_ge(gate_act, g + 1)
                tt(sgate[:, :, :], sgate[:, :, :], rbc[:, :].unsqueeze(1).broadcast_to([P, 2, T]), mul).then_inc(gate_r, 1)

            def up_evac(g):
                dve.wait_ge(gate_r, g + 1)
                dve.wait_ge(pe_used, 8 * g + FF_C0 + 8)
                if not isinstance(g, int) or g > 0:
                    dve.wait_ge(nz_lo, g + 8)
                tt(hidF[:, :, :], sgate[:, :, :], acc(1), mul).then_inc(drained[1], 1)

            def hid_lo_(g):
                dve.wait_ge(ff_hi, g + 1)
                tt(hid_lo[:, ds(2 * g, 2)], hidF[:, :, :], hid_hi[:, ds(2 * g, 2)].bitcast(F32), sub).then_inc(nz_lo, 1)

            for i in range(8):
                lo(FF_C0 + i + AHEAD, (i + AHEAD) % RING)
                if i == 0:
                    input_lo(3)
                if i == 5:
                    dve.wait_ge(nz_r, 4)
                    gate_scale(0)
                if i == 7:
                    gate_times_r(0)
            dve.wait_ge(tl_out, 16 * 20)
            with dve.Fori(1, FF_PAIRS) as g:
                for i in range(8):
                    lo(8 * g + FF_C0 + i + AHEAD, (i + AHEAD) % RING)
                    if i == 0:
                        up_evac(g - 1)
                    if i == 2:
                        hid_lo_(g - 1)
                    if i == 4:
                        gate_scale(g)
                    if i == 6:
                        gate_times_r(g)
            up_evac(FF_PAIRS - 1)
            hid_lo_(FF_PAIRS - 1)
            for c in range(AHEAD, DOWN_GROUPS * DOWN_CH):
                lo(DOWN_C0 + c, c % RING)
            dve.wait_ge(o_r, 4)
            dve.wait_ge(drained[1], 44)
            for q in range(3):
                scale_quarter(1, q, ffg)
            for q in range(3):
                add_quarter(1, q, ffg, ffg)


_INS = ["x_prompt", "x_sample", "state_hgrn", "state_gdn", "state_gdn_conv", "state_rglru_h", "state_rglru_conv",
        "ln_mix_pre", "ln_mix_post", "ln_ffn_pre", "ln_ffn_post", "w_in", "w_out", "a_norm",
        "b_conv_w", "b_A_log", "b_dt_bias", "b_norm", "c_conv_w", "c_conv_b", "c_wa", "c_ba", "c_wx", "c_bx", "c_lam",
        "w_gate", "w_up", "w_down"]
_OUTS = [(1, 256, 2048), (8, 1, 2048), (1, 1, 4, 128, 128), (1, 8, 4, 128, 128), (1, 1, 8, 128, 128),
         (1, 8, 8, 128, 128), (1, 1, 3, 3072), (1, 8, 3, 3072), (1, 1, 512), (1, 8, 512), (1, 1, 3, 512), (1, 8, 3, 512)]


def kernel(**inputs):
    import numpy as _np
    import concourse.bacc as _bacc
    from concourse import mybir as _mybir
    from concourse.bass_utils import run_bass_kernel_spmd as _run

    nc = _bacc.Bacc("TRN2", target_bir_lowering=False, num_devices=1)
    arrays, args = {}, []
    for name in _INS:
        a = _np.ascontiguousarray(inputs[name])
        arrays[f"in_{name}_dram"] = a
        args.append(nc.dram_tensor(f"in_{name}_dram", a.shape, _mybir.dt.from_np(a.dtype), kind="ExternalInput").ap())
    for i, shape in enumerate(_OUTS):
        args.append(nc.dram_tensor(f"out_{i}_dram", shape, _mybir.dt.float32, kind="ExternalOutput").ap())
    hybrid_layer(nc, *args)
    r = _run(nc, [arrays], core_ids=[0])
    return tuple(r.results[0][f"out_{i}_dram"] for i in range(len(_OUTS)))
```

```python
from contextlib import ExitStack
from math import log

import concourse.bass as bass
from concourse import mybir

F32 = mybir.dt.float32
F32R = mybir.dt.float32r
ALU = mybir.AluOpType
ACT = mybir.ActivationFunctionType
AX = mybir.AxisListType
ds = bass.ds

P = 128
L = 256
NB = 8
T = L + NB
D = 2048
KT = D // P
FF = 5632
FT = FF // P
EPS = 1e-6
CK = 4
CC = 256
RING = 4
AHEAD = RING - 1
SLOTS = 16
GATE_OFF = 6144
C_OFF = 6160
LEVELS = 7
CONVW = 4
XW = 3 + L + NB * CONVW
CW = XW - 3
B_ROUNDS, A_ROUNDS = 4, 2
ROUNDS = B_ROUNDS + A_ROUNDS + 1
OUT_GROUPS, FF_PAIRS, DOWN_GROUPS = 8, 22, 8
OUT_C0 = ROUNDS * SLOTS
FF_C0 = OUT_C0 + OUT_GROUPS * 4
DOWN_C0 = FF_C0 + FF_PAIRS * 8
DOWN_CH = FT // CK
CHUNKS = DOWN_C0 + DOWN_GROUPS * DOWN_CH
OUT_START = [(0, 1), (0, 2), (1, 1), (1, 2), (0, 0), (1, 0), (0, 3), (1, 3)]
OUT_G0, FF_G0, DOWN_G0 = 28, 36, 80
G_MIX_PRE, G_MIX_POST, G_FFN_PRE, G_FFN_POST, RG_H, C_CONV = 0, 16, 32, 48, 64, 96
B_CONV, C_BIAS, C_BA, C_BX, C_LAM, A_NORM, B_NORM, C_HIST = 112, 208, 212, 216, 220, 224, 225, 226
PCOLS = 322
F_B, F_BETA, F_BETAEXP, F_KEND, F_EEND, F_G = range(6)
Y_ORDER = (0, 1, 3, 2)
TURN_BANKS = (4, 5, 7)
SERIES = [1 / 15, 1 / 13, 1 / 11, 1 / 9, 1 / 7, 1 / 5, 1 / 3, 1.0]


def hybrid_layer(nc, x_prompt, x_sample, state_hgrn, state_gdn, state_gdn_conv, state_rglru_h, state_rglru_conv,
                 ln_mix_pre, ln_mix_post, ln_ffn_pre, ln_ffn_post, w_in, w_out, a_norm,
                 b_conv_w, b_A_log, b_dt_bias, b_norm, c_conv_w, c_conv_b, c_wa, c_ba, c_wx, c_bx, c_lam,
                 w_gate, w_up, w_down,
                 y_prompt, y_sample, o_hgrn_p, o_hgrn_s, o_gdn_p, o_gdn_s, o_gconv_p, o_gconv_s,
                 o_rh_p, o_rh_s, o_rconv_p, o_rconv_s):
    with ExitStack() as ctx:
        at = [16640]
        place = {}

        def put(name, shape, dt=F32, offset=None):
            size = 4
            for s in shape[1:]:
                size *= s
            if offset is None:
                offset = at[0]
                at[0] += -(-size // 32) * 32
            assert offset + size <= 229368, (name, offset + size)
            place[name] = offset
            return nc.alloc_sbuf_tensor_at(name, [*shape], dt, offset=offset)

        def sem(name):
            return ctx.enter_context(nc.semaphore(name))

        xT = put("xT", [P, KT, T])
        act_hi = put("act_hi", [P, KT, T], F32R)
        act_lo = put("act_lo", [P, KT, T], F32R)
        raw = put("raw", [P, RING, CK, CC])
        w_hi = put("w_hi", [P, RING, CK, CC], F32R)
        w_lo = put("w_lo", [P, RING, CK, CC], F32R)
        masks = put("masks", [P, 1 + LEVELS, P])
        upper = put("upper", [P, P])
        ones = put("ones", [P, P])
        params = put("params", [P, PCOLS])
        consts = put("consts", [P, 4])
        rbc = put("rbc", [P, T])
        ident = masks[:, 0, :]
        eps = consts[:, 0:1]

        overlay = at[0]
        cat_hi = put("cat_hi", [P, KT, T], F32R)
        cat_lo = put("cat_lo", [P, KT, T], F32R)
        qkv = put("qkv", [P, 4, 2, T])
        xraw = put("xraw", [P, 2, 2, XW])
        conv = put("conv", [P, 2, CW])
        convw = put("convw", [P, 2, 2, CONVW])
        tail_b = put("tail_b", [P, 3 + NB, 24])
        tail_c = put("tail_c", [P, 11 + 9, 4])
        hist_b = put("hist_b", [P, NB, 3, 24])
        gates = put("gates", [P, 6, 4, 4])
        sgates = put("sgates", [P, 2, 4, 16])
        lamc = put("lamc", [P, 2, 4])
        pair = put("pair", [P, 6, 4])
        spair = put("spair", [P, 2, 16])
        small = put("small", [P, 6, 16])
        S = put("S", [P, 2, 2, P])
        sq = put("sq", [P, 4, T])
        rs = put("rs", [P, 4, T])
        nrm = put("nrm", [P, 2, 2, T])
        oT = put("oT", [P, 2, T])
        nwT = put("nwT", [P, 2, P])
        decay = put("decay", [P, 4, P])
        eb = put("eb", [P, 4, P])
        kb = put("kb", [P, 4, P])
        k_end = put("k_end", [P, 4, P])
        kbe = put("kbe", [P, 4, P])
        vb = put("vb", [P, 4, P])
        AT = put("AT", [P, 4, P])
        QK = put("QK", [P, 4, P])
        TT = put("TT", [P, 4, P])
        u = put("u", [P, 4, P])
        Ss = put("Ss", [P, 16, P])
        sqv = sq[:, :, :].rearrange("p a t -> p (a t)")
        rsv = rs[:, :, :].rearrange("p a t -> p (a t)")
        AL = sqv[:, 0:512].rearrange("p (x t) -> p x t", x=4)
        XM = rsv[:, 0:512].rearrange("p (x t) -> p x t", x=4)
        TM = rsv[:, 512:1024].rearrange("p (x t) -> p x t", x=4)
        lev = put("lev", [P, LEVELS, 512], offset=place["decay"])
        prod = sqv[:, 0:1024].rearrange("p (l t) -> p l t", l=8)
        attT = TT
        qA = u[:, :, :].rearrange("p (j c) t -> p j (c t)", j=2)
        q_s = small[:, 2, :]
        v_s = small[:, 4, :]
        bA = sqv[:, 0:512].rearrange("p (x t) -> p x t", x=4)
        kend_f = sqv[:, 512:1024].rearrange("p (x t) -> p x t", x=4)
        v_tm = rsv[:, 0:512].rearrange("p (x t) -> p x t", x=4)
        ke_tm = rsv[:, 512:1024].rearrange("p (x t) -> p x t", x=4)
        ca = put("ca", [P, 4, T], offset=place["decay"])
        cth = put("cth", [P, 4, T], offset=place["decay"] + 4 * 4 * T)
        cm = put("cm", [P, 4, T], offset=place["decay"] + 8 * 4 * T)
        wbd = put("wbd", [P, 2, 4, P])
        xtok = [put("xtok0", [P, D], offset=place["kb"]), put("xtok1", [P, D], offset=place["sq"]),
                put("xtok2", [P, D], offset=place["AT"])]
        xn = put("xn", [P, 3, D], offset=place["cat_hi"])
        hF = put("hF", [P, KT, T], offset=place["cat_hi"])
        stage = put("stage", [P, 8, P], offset=place["nrm"])
        bab = put("bab", [16, T], offset=place["decay"])
        gw = put("gw", [P, KT, 16], offset=place["cat_hi"] + 12 * D)
        gw_hi = put("gw_hi", [P, KT, 16], F32R, offset=place["cat_hi"] + 12 * D + 1024)
        gw_lo = put("gw_lo", [P, KT, 16], F32R, offset=place["cat_hi"] + 12 * D + 2048)
        xss = put("xss", [P, 2, 3], offset=place["decay"] + 3840)
        gt = put("gt", [P, 3, 16], offset=place["decay"] + 2048)
        zz = put("zz", [P, 6, 28], offset=place["decay"] + 2304)
        sel = put("sel", [8, 2, 8, 8], offset=place["decay"] + 3072)
        bcA = put("bcA", [P, 8], offset=place["decay"] + 3648)
        bcD = put("bcD", [P, 8], offset=place["decay"] + 3680)
        gb = put("gb", [P, 2, 16], offset=place["decay"] + 3712)
        mixg = put("mixg", [P, KT, T], offset=place["decay"])
        rows = put("rows", [P, 4, P], offset=place["sq"])
        hid_hi = put("hid_hi", [P, FT, T], F32R, offset=overlay)
        hid_lo = put("hid_lo", [P, FT, T], F32R, offset=overlay + FT * T * 4)
        after = overlay + 2 * FT * T * 4
        sqo = put("sqo", [P, 2, 2, T], offset=after)
        sacc = put("sacc", [P, 2, T], offset=after + 32 * T)
        sgate = put("sgate", [P, 2, T], offset=after + 16 * T)
        hidF = put("hidF", [P, 2, T], offset=after + 24 * T)
        ffg = put("ffg", [P, KT, T], offset=place["act_lo"])
        ytok = put("ytok", [P, 3, D], offset=overlay)

        ps = ctx.enter_context(nc.psum_tensor("ps", [P, 8, 512], F32))

        def acc(par):
            return ps[:, 2 * par:2 * par + 2, 0:T]

        def quad(bank):
            return ps[:, bank, :].rearrange("p (x t) -> p x t", x=4)

        raw_in = [sem(f"raw_in{i}") for i in range(RING)]
        hi_done = sem("hi_done")
        lo_done = sem("lo_done")
        pe_used = sem("pe_used")
        drained = [sem("drained0"), sem("drained1")]
        g_done = sem("g_done")
        raw_q = sem("raw_q")
        hist_in = sem("hist_in")
        conv_done = sem("conv_done")
        silu_done = sem("silu_done")
        x_in = [sem(f"x_in{t}") for t in range(3)]
        par0_in = sem("par0_in"); par_in = sem("par_in")
        gw_in = sem("gw_in"); bc_in = sem("bc_in"); wbd_in = sem("wbd_in")
        x_ss = sem("x_ss")
        x_n = sem("x_n")
        xn_pe = sem("xn_pe")
        xn_hi = sem("xn_hi"); xn_lo = sem("xn_lo")
        raw_pe = sem("raw_pe"); raw_cp = sem("raw_cp")
        par0_pe = sem("par0_pe"); gain_in = sem("gain_in")
        gw_s = sem("gw_s")
        pool_c = sem("pool_c")
        st_pe = sem("st_pe"); st_dve = sem("st_dve"); st_act = sem("st_act")
        nz_sq = sem("nz_sq"); nz_acc = sem("nz_acc")
        nz_pe = sem("nz_pe"); nz_r = sem("nz_r")
        nz_hi = sem("nz_hi"); nz_lo = sem("nz_lo")
        mx = {n: sem("mx_" + n) for n in (
            "pair",
            "sq",
            "ss",
            "ln",
            "rs",
            "nrm",
            "bc",
            "tr",
            "eb",
            "kb",
            "d",
            "dec",
            "cau",
            "tm",
            "qe",
            "g",
            "at",
            "al",
            "tt",
            "t1",
            "t",
            "x",
            "xc",
            "p",
            "u0",
            "u0c",
            "s1",
            "s1c",
            "u1",
            "u1c",
            "so",
            "s2",
            "oc",
            "ks",
            "qkp",
            "qk",
            "us",
            "sdec",
            "ub",
            "sn",
            "os",
            "osq",
            "oss",
            "oln",
            "ors",
            "og",
            "ohi",
            "olo",
            "ld",
            "st",
        )}
        a_ = {n: sem("ha_" + n) for n in (
            "ln",
            "lf",
            "k",
            "q",
            "b",
            "d",
            "e",
            "ex",
            "fs",
            "w",
            "wp",
            "tr",
            "tm",
            "at",
            "pr",
            "rd",
            "vs",
        )}
        c_ = {n: sem("rg_" + n) for n in (
            "r",
            "i",
            "prei",
            "ix",
            "a",
            "x",
            "h",
            "hi",
            "lo",
        )}
        o_sq = sem("o_sq"); o_acc = sem("o_acc")
        o_pe = sem("o_pe"); o_r = sem("o_r")
        o_g = sem("o_g"); o_y = sem("o_y")
        o_h = sem("o_h")
        o_pool = sem("o_pool")
        tl_pe = sem("tl_pe"); tl_cp = sem("tl_cp"); tl_out = sem("tl_out"); old_out = sem("old_out")
        gate_act = sem("gate_act"); gate_r = sem("gate_r"); ff_hi = sem("ff_hi")
        y_pe = sem("y_pe"); y_cp = sem("y_cp"); y_out = sem("y_out")

        block = ctx.enter_context(nc.Block())

        @block.sync
        def _(sp):
            w_in_v = w_in[0].rearrange("(k p) n -> p k n", p=P)
            w_out_v = w_out[0].rearrange("(k p) n -> p k n", p=P)
            w_gate_v = w_gate[0].rearrange("(k p) n -> p k n", p=P)
            w_up_v = w_up[0].rearrange("(k p) n -> p k n", p=P)
            w_down_v = w_down[0].rearrange("(k p) n -> p k n", p=P)

            def load(c, slot, src, first=False):
                if not first:
                    sp.wait_ge(lo_done, c - RING + 1)
                sp.dma_start(raw[:, slot], src).then_inc(raw_in[slot], 16)

            def in_group(c0, col, first=False):
                for i in range(4):
                    load(c0 + i, i, w_in_v[:, 4 * i:4 * i + 4, col], first)

            sp.dma_start(xtok[2][0:NB, :], x_sample[:, 0, :]).then_inc(x_in[2], 16)
            for t in range(2):
                sp.dma_start(xtok[t][:, :], x_prompt[0, t * P:(t + 1) * P, :]).then_inc(x_in[t], 16)
            for n, a in enumerate((ln_mix_pre, ln_mix_post, ln_ffn_pre, ln_ffn_post)):
                sp.dma_start(stage[16 * n:16 * n + 16, 0], a.rearrange("o (k p) -> (o k) p", p=P)).then_inc(par0_in, 16)
            sp.dma_start(stage[64:96, 0], state_rglru_h[0].rearrange("b (k p) -> (b k) p", p=P)).then_inc(par0_in, 16)
            sp.dma_start(stage[96:112, 0], c_conv_w[0].rearrange("j (k p) -> (j k) p", p=P)).then_inc(par0_in, 16)
            b_col = [2048, 3072, 4096, 5120]
            in_group(0, slice(b_col[0], b_col[0] + CC), first=True)
            sp.dma_start(stage[0:96, 1], b_conv_w[0].rearrange("j (k p) -> (j k) p", p=P)).then_inc(par_in, 16)
            for n, a in enumerate((c_conv_b, c_ba, c_bx, c_lam)):
                sp.dma_start(stage[96 + 4 * n:100 + 4 * n, 1], a.rearrange("o (k p) -> (o k) p", p=P))\
                    .then_inc(par_in, 16)
            sp.dma_start(stage[112:113, 1], a_norm).then_inc(par_in, 16)
            sp.dma_start(stage[113:114, 1], b_norm).then_inc(par_in, 16)
            sp.dma_start(stage[0:96, 2], state_rglru_conv[0].rearrange("b j (k p) -> (b j k) p", p=P))\
                .then_inc(par_in, 16)
            hist = state_gdn_conv[0].rearrange("b j (k p) -> (b j k) p", p=P)
            for n in range(4):
                sp.dma_start(stage[:, 3 + n], hist[P * n:P * n + P, :]).then_inc(par_in, 16)
            sp.dma_start(stage[0:64, 7], hist[512:576, :]).then_inc(par_in, 16)
            sp.dma_start(gw[:, :, :], w_in_v[:, :, GATE_OFF:GATE_OFF + 16]).then_inc(gw_in, 16)
            sp.dma_start(bcA[:, :], b_A_log.broadcast_to([P, 8])).then_inc(bc_in, 16)
            sp.dma_start(bcD[:, :], b_dt_bias.broadcast_to([P, 8])).then_inc(bc_in, 16)
            for q in range(1, 4):
                in_group(4 * q, slice(b_col[q], b_col[q] + CC))
            with sp.Fori(1, B_ROUNDS) as r:
                for q in range(4):
                    in_group(SLOTS * r + 4 * q, ds(r * CC + b_col[q], CC))
            for r in range(A_ROUNDS):
                for q in range(4):
                    in_group(SLOTS * (B_ROUNDS + r) + 4 * q, slice(512 * q + CC * r, 512 * q + CC * r + CC))
            for q in range(4):
                in_group(SLOTS * (ROUNDS - 1) + 4 * q, slice(C_OFF + CC * q, C_OFF + CC * q + CC))
            for s, (g, i) in enumerate(OUT_START):
                load(OUT_C0 + s, s % RING, w_out_v[:, 4 * i:4 * i + 4, g * CC:g * CC + CC])
            with sp.Fori(2, OUT_GROUPS) as g:
                for i in range(4):
                    load(4 * g + OUT_C0 + i, i, w_out_v[:, 4 * i:4 * i + 4, ds(g * CC, CC)])
            with sp.Fori(0, FF_PAIRS) as g:
                for n, w in enumerate((w_gate_v, w_up_v)):
                    for i in range(4):
                        load(8 * g + FF_C0 + 4 * n + i, i, w[:, 4 * i:4 * i + 4, ds(g * CC, CC)])
            with sp.Fori(0, 2) as h:
                for g in range(4):
                    for i in range(DOWN_CH):
                        c = DOWN_CH * g + i
                        load(44 * h + DOWN_C0 + c, c % RING, w_down_v[:, CK * i:CK * i + CK, ds(h * 1024 + g * CC, CC)])
            for i, q in enumerate(Y_ORDER):
                cols = slice(512 * q, 512 * q + 512)
                for t, n in enumerate((P, P, NB)):
                    dst = y_prompt[0, t * P:(t + 1) * P, cols] if t < 2 else y_sample[:, 0, cols]
                    sp.wait_ge(y_cp, 3 * i + t + 1)
                    sp.dma_start(dst, ytok[0:n, t, cols]).then_inc(y_out, 16)
            sp.wait_ge(y_out, 16 * 12)

        @block.gpsimd
        def _(pool):
            steps = [0]
            passed = sem("passed")

            def const(ins):
                ins.then_inc(pool_c, 1)
                steps[0] += 1
                pool.wait_ge(pool_c, steps[0])

            const(pool.memset(masks[:, :, :], 0.0))
            const(pool.memset(ones[:, :], 1.0))
            const(pool.memset(upper[:, :], 1.0))
            const(pool.memset(consts[:, :], EPS))
            const(pool.memset(zz[:, :, :], 0.0))
            const(pool.memset(gt[:, :, :], 0.0))
            const(pool.affine_select(out=ident, in_=ident, compare_op=ALU.not_equal, fill=1.0, base=0,
                                     pattern=[[-1, P]], channel_multiplier=1))
            const(pool.affine_select(out=upper[:, :], in_=upper[:, :], compare_op=ALU.is_ge, fill=0.0, base=0,
                                     pattern=[[1, P]], channel_multiplier=-1))
            assert steps[0] == 8
            for l in range(1, LEVELS + 1):
                m = 1 << (l - 1)
                mv = masks[:, l, :].rearrange("p (n h m) -> p n h m", h=2, m=m)
                const(pool.memset(mv[:, :, 1, :], 1.0))
                v = masks[:, l, :].rearrange("p (n w) -> p n w", w=2 * m)
                const(pool.affine_select(out=v, in_=v, compare_op=ALU.is_ge, fill=0.0, base=0,
                                         pattern=[[-2 * m, P // (2 * m)], [0, 2 * m]], channel_multiplier=1))
                const(pool.affine_select(out=v, in_=v, compare_op=ALU.is_ge, fill=0.0, base=m - 1,
                                         pattern=[[2 * m, P // (2 * m)], [0, 2 * m]], channel_multiplier=-1))
            pool.dma_start(o_gconv_s[0, :, 0:2, :], state_gdn_conv[0, :, 1:3, :]).then_inc(old_out, 16)
            pool.dma_start(o_rconv_s[0, :, 0:2, :], state_rglru_conv[0, :, 1:3, :]).then_inc(old_out, 16)
            const(pool.memset(xraw[:, :, :, 0:3], 0.0))

            def history(n, slot, tile0, is_c=False):
                if not isinstance(n, int) or n > 0:
                    pool.wait_ge(conv_done, n)
                hv = params[:, C_HIST:C_HIST + 96].rearrange("p (b j k) -> p b j k", j=3, k=4) if is_c else hist_b
                wv = params[:, C_CONV:C_CONV + 16].rearrange("p (j k) -> p j k", k=4) if is_c else \
                    params[:, B_CONV:B_CONV + 96].rearrange("p (j k) -> p j k", k=24)
                for t in range(2):
                    dst = xraw[:, slot, t, 3 + L:XW].rearrange("p (b j) -> p b j", j=CONVW)
                    src = hv[:, :, :, ds(tile0 + t, 1)].rearrange("p b j o -> p b (j o)")
                    pool.tensor_copy(dst[:, :, 0:3], src).then_inc(hist_in, 1)
                    pool.tensor_copy(convw[:, slot, t, :], wv[:, :, ds(tile0 + t, 1)].rearrange("p j o -> p (j o)"))\
                        .then_inc(hist_in, 1)

            def settled():
                pool.sem_inc(passed, 1)

            def states(n, k, src):
                if not isinstance(n, int) or n > 0:
                    pool.wait_ge(mx["st"], 64 * n)
                settled()
                for j in range(2):
                    pool.dma_start(Ss[:, 8 * j:8 * j + 8, :],
                                   src[0, :, ds(2 * k + j, 1)].rearrange("b o d e -> d (b o) e")).then_inc(mx["ld"], 16)

            def store(n, k, dst_s, dst_p):
                pool.wait_ge(mx["sn"], 16 * n + 16)
                pool.wait_ge(mx["s2"], 2 * n + 2)
                settled()
                for j in range(2):
                    pool.dma_start(dst_s[0, :, ds(2 * k + j, 1)].rearrange("b o d e -> d (b o) e"),
                                   Ss[:, 8 * j:8 * j + 8, :]).then_inc(mx["st"], 16)
                    pool.dma_start(dst_p[0, 0, ds(2 * k + j, 1)].rearrange("o d e -> d (o e)"),
                                   S[:, j, 1, :]).then_inc(mx["st"], 16)

            def b_mixer(n, between=None):
                states(n, n, state_gdn)
                pool.wait_ge(mx["dec"], n + 1)
                pool.tensor_tensor(decay[:, :, :], decay[:, :, :],
                                   upper[:, :].unsqueeze(1).broadcast_to([P, 4, P]), ALU.mult).then_inc(mx["cau"], 1)
                pool.wait_ge(mx["ld"], 32 * n + 32)
                pool.wait_ge(mx["ks"], n + 1)
                pool.wait_ge(mx["pair"], 2 * n + 2)
                pool.tensor_tensor(Ss[:, :, :], Ss[:, :, :], spair[:, 0, :].unsqueeze(2).broadcast_to([P, 16, P]),
                                   ALU.mult).then_inc(mx["sdec"], 1)
                pool.wait_ge(mx["at"], 2 * n + 2)
                for l in range(2, LEVELS + 1):
                    if l == 5 and between:
                        between()
                    if l == 2:
                        pool.wait_ge(mx["tt"], n + 1)
                    else:
                        pool.wait_ge(mx["x"], 6 * n + l - 2)
                    pool.tensor_tensor(AL, AT[:, :, :], masks[:, l, :].unsqueeze(1).broadcast_to([P, 4, P]),
                                       ALU.mult).then_inc(mx["al"], 1)
                store(n, n, o_gdn_s, o_gdn_p)

            def a_mixer(n, k):
                if k:
                    pool.wait_ge(a_["vs"], k)
                states(n, k, state_hgrn)
                pool.wait_ge(mx["ld"], 32 * n + 32)
                pool.wait_ge(a_["fs"], k + 1)
                pool.tensor_tensor(Ss[:, :, :], Ss[:, :, :], small[:, 0, :].unsqueeze(2).broadcast_to([P, 16, P]),
                                   ALU.mult).then_inc(mx["sdec"], 1)
                pool.wait_ge(a_["ex"], 6 * k + 6)
                pool.wait_ge(a_["k"], k + 1)
                two = lambda a: a.rearrange("p (j c) t -> p j (c t)", j=2)
                pool.tensor_tensor(two(kend_f), two(kend_f), nrm[:, 0, :, 0:L], ALU.mult).then_inc(a_["wp"], 1)
                pool.wait_ge(a_["q"], 3 * k + 3)
                pool.tensor_tensor(nwT[:, :, :], nwT[:, :, :], qA[:, :, P:L], ALU.mult).then_inc(a_["wp"], 1)
                store(n, k, o_hgrn_s, o_hgrn_p)

            const(pool.memset(wbd[:, :, :, :], 0.0))
            for w, src in enumerate((c_wa, c_wx)):
                for h in range(2):
                    pool.dma_start(wbd[64 * h:64 * h + 64, w, :, 64 * h:64 * h + 64],
                                   src[0, h:8:2].rearrange("n i j -> i n j")).then_inc(wbd_in, 16)
            pool.wait_ge(st_dve, 6)
            history(0, 0, 0)
            history(0, 1, 8)
            history(1, 0, 16)

            def b_round(r):
                history(3 * r, 0, 2 * r)
                history(3 * r, 1, 2 * r + 8)
                b_mixer(r - 1, lambda: history(3 * r + 1, 0, 2 * r + 16))

            b_round(1)
            with pool.Fori(2, B_ROUNDS) as r:
                b_round(r)
            history(12, 0, 0, is_c=True)
            history(12, 1, 2, is_c=True)
            b_mixer(3)
            a_mixer(4, 0)
            a_mixer(5, 1)
            pool.wait_ge(c_["prei"], 8)
            pool.tensor_tensor(rs[:, :, :], rs[:, :, :], qkv[:, 0:2].rearrange("p a j t -> p (a j) t"), ALU.mult)\
                .then_inc(c_["ix"], 1)
            pool.wait_ge(tl_cp, 4)
            pool.dma_start(o_gconv_p[0, 0].rearrange("j (k p) -> (j k) p", p=P), rows[0:72, 0]).then_inc(tl_out, 16)
            for b in range(NB):
                src = rows[24 * b:24 * b + 24, 1] if b < 5 else rows[24 * (b - 5):24 * (b - 5) + 24, 2]
                pool.dma_start(o_gconv_s[0, b, 2].rearrange("(k p) -> k p", p=P), src).then_inc(tl_out, 16)
            pool.dma_start(o_rconv_p[0, 0].rearrange("j (k p) -> (j k) p", p=P), rows[0:12, 3]).then_inc(tl_out, 16)
            for b in range(NB):
                pool.dma_start(o_rconv_s[0, b, 2].rearrange("(k p) -> k p", p=P),
                               rows[12 + 4 * b:16 + 4 * b, 3]).then_inc(tl_out, 16)
            pool.dma_start(o_rh_p[0, 0].rearrange("(k p) -> k p", p=P), rows[44:48, 3]).then_inc(tl_out, 16)
            pool.dma_start(o_rh_s[0].rearrange("b (k p) -> (b k) p", p=P), rows[48:80, 3]).then_inc(tl_out, 16)

            def residual_pool(n, src, dst, base):
                pool.wait_ge(o_r, 2 * n + 2)
                pool.wait_ge(drained[1], base)
                s = slice(12, 16)
                pool.tensor_tensor(src[:, s], src[:, s], rbc[:, :].unsqueeze(1).broadcast_to([P, 4, T]), ALU.mult)\
                    .then_inc(o_pool, 1)
                pool.wait_ge(o_pool, 2 * n + 1)
                pool.tensor_tensor(dst[:, s], xT[:, s], src[:, s], ALU.add).then_inc(o_pool, 1)

            residual_pool(0, mixg, xT, 18)
            residual_pool(1, ffg, ffg, 44)
            pool.wait_ge(tl_out, 16 * 20)
            pool.wait_ge(old_out, 32)
            pool.wait_ge(mx["st"], 64 * 6)

        @block.tensor
        def _(pe):
            def chunk(c, slot, par, k0, nk, x_hi, x_lo, half=None, begin=0):
                if half != 1:
                    pe.wait_ge(lo_done, c + 1)
                for m in range(2):
                    if half is not None and m != half:
                        continue
                    for k in range(CK):
                        out = ps[:, 2 * par + m, 0:T]
                        wh, wl = w_hi[:, slot, k, m * P:m * P + P], w_lo[:, slot, k, m * P:m * P + P]
                        kk = k0 + k
                        pe.matmul(out, wh, x_hi[:, kk], start=(kk == begin), stop=False)
                        pe.matmul(out, wh, x_lo[:, kk], start=False, stop=False)
                        last = pe.matmul(out, wl, x_hi[:, kk], start=False, stop=(kk == nk - 1))
                if half != 0:
                    last.then_inc(pe_used, 1)

            def bank_free(par, n):
                if not isinstance(n, int) or n > 0:
                    pe.wait_ge(drained[par], n)

            pe.wait_ge(pool_c, 8)
            pe.wait_ge(par0_in, 6 * 16)
            pe.transpose(ps[:, 6, 0:112], stage[0:112, 0], ident[0:112, 0:112]).then_inc(par0_pe, 1)

            def turn_input(q):
                for k in range(4 * q, 4 * q + 4):
                    if k >= 4:
                        pe.wait_ge(xn_lo, k - 3)
                    for t, n in enumerate((P, P, NB)):
                        last = pe.transpose(ps[:, 2 + k % 4, t * P:t * P + n], xn[0:n, t, k * P:k * P + P],
                                            ident[0:n, 0:n])
                    last.then_inc(xn_pe, 1)

            def turn_params():
                pe.wait_ge(par_in, 13 * 16)
                pe.wait_ge(gain_in, 1)
                for i, (n, bank, col) in enumerate(((114, 6, 112), (96, 6, 226), (P, 7, 0), (P, 7, P),
                                                    (P, 7, 2 * P), (P, 7, 3 * P), (64, 4, 0))):
                    last = pe.transpose(ps[:, bank, col:col + n], stage[0:n, i + 1], ident[0:n, 0:n])
                last.then_inc(st_pe, 1)

            def turn_x(q):
                t, k0 = q // 4, 4 * (q % 4)
                n = P if t < 2 else NB
                if q >= 3:
                    pe.wait_ge(raw_cp, q - 2)
                for k in range(4):
                    last = pe.transpose(ps[:, TURN_BANKS[q % 3], k * P:k * P + n],
                                        xtok[t][0:n, (k0 + k) * P:(k0 + k) * P + P], ident[0:n, 0:n])
                last.then_inc(raw_pe, 1)

            def input_sum():
                pe.wait_ge(nz_acc, 3)
                for k in range(4):
                    last = pe.matmul(ps[:, 5, 0:T], ones[:, :], hF[:, k], start=(k == 0), stop=(k == 3))
                last.then_inc(nz_pe, 1)

            def gate_columns():
                pe.wait_ge(gw_s, 2)
                pe.wait_ge(st_dve, 3)
                out = ps[0:16, 7, 0:T]
                for k in range(KT):
                    pe.matmul(out, gw_hi[:, k], act_hi[:, k], start=(k == 0), stop=False)
                    pe.matmul(out, gw_hi[:, k], act_lo[:, k], start=False, stop=False)
                    last = pe.matmul(out, gw_lo[:, k], act_hi[:, k], start=False, stop=(k == KT - 1))
                last.then_inc(st_pe, 1)

            def turn_gates():
                pe.wait_ge(st_dve, 7)
                for t in range(3):
                    n = P if t < 2 else NB
                    last = pe.transpose(ps[0:n, 6, 16 * t:16 * t + 16], bab[0:16, t * P:t * P + n], ident[0:16, 0:16])
                last.then_inc(st_pe, 1)

            def gating():
                pe.wait_ge(st_dve, 31)
                g2 = gt[:, 0:2, 8:16]
                pe.matmul(ps[:, 6, 64:80], upper[:, :], g2, start=True, stop=True)
                pe.matmul(ps[:, 6, 80:96], ones[:, :], g2, start=True, stop=True)
                pe.matmul(ps[:, 6, 128:256], ones[0:8, :], sel[:, :, :, :], start=True, stop=True).then_inc(st_pe, 1)

            def b_step(hp, n):
                if hp == 1:
                    pe.wait_ge(mx["sq"], n + 1)
                    if not isinstance(n, int) or n > 0:
                        pe.wait_ge(mx["ors"], n)
                    for i in range(4):
                        last = pe.matmul(ps[:, 4 + i, 0:T], ones[:, :], sq[:, i], start=True, stop=True)
                    last.then_inc(mx["ss"], 1)
                if hp == 3:
                    pe.wait_ge(mx["ln"], n + 1)
                    pe.wait_ge(mx["pair"], 2 * n + 2)
                    for x in range(4):
                        pe.matmul(ps[:, 4, x * P:x * P + P], pair[:, F_G, x:x + 1].broadcast_to([P, P]), upper[:, :],
                                  start=True, stop=True)
                    for x in range(4):
                        pe.matmul(ps[:, 5, x * P:x * P + P], pair[:, F_BETA, x:x + 1].broadcast_to([P, P]), ident,
                                  start=True, stop=True)
                    for x in range(4):
                        last = pe.transpose(ps[:, 7, x * P:x * P + P],
                                            qkv[:, 2, x // 2, (x % 2) * P:(x % 2) * P + P], ident)
                    last.then_inc(mx["bc"], 1)
                if hp == 5:
                    pe.wait_ge(mx["nrm"], 2 * n + 2)
                    for x in range(4):
                        last = pe.transpose(ps[:, 6, x * P:x * P + P],
                                            nrm[:, 1, x // 2, (x % 2) * P:(x % 2) * P + P], ident)
                    last.then_inc(mx["tr"], 1)
                if hp == 6:
                    pe.wait_ge(mx["ld"], 32 * n + 32)
                    pe.wait_ge(mx["tm"], 3 * n + 3)
                    for x in range(16):
                        last = pe.matmul(ps[:, 7, 2 * x:2 * x + 2], Ss[:, x, :],
                                         nrm[:, :, x // 8, L + x % 8], start=True, stop=True)
                    last.then_inc(mx["ks"], 1)
                if hp == 7:
                    pe.wait_ge(mx["kb"], n + 1)
                    pe.wait_ge(mx["eb"], n + 1)
                    pe.wait_ge(mx["d"], 2 * n + 2)
                    for x in range(4):
                        kn = nrm[:, 1, x // 2, (x % 2) * P:(x % 2) * P + P]
                        pe.matmul(ps[:, 4, x * P:x * P + P], kn, kb[:, x, :], start=True, stop=True)
                        last = pe.matmul(ps[:, 5, x * P:x * P + P], kn,
                                         nrm[:, 0, x // 2, (x % 2) * P:(x % 2) * P + P], start=True, stop=True)
                    last.then_inc(mx["g"], 1)
                if hp == 8:
                    pe.wait_ge(mx["qkp"], n + 1)
                    pe.matmul(ps[:, 7, 32:48], ones[:, :], small[:, 0, :], start=True, stop=True).then_inc(mx["qk"], 1)
                if hp == 10:
                    pe.wait_ge(mx["tt"], n + 1)
                    for x in range(4):
                        last = pe.transpose(ps[:, 6, x * P:x * P + P], TT[:, x, :], ident)
                    last.then_inc(mx["t1"], 1)
                if 12 <= hp <= 23:
                    l = 2 + (hp - 12) // 2
                    if hp % 2 == 0:
                        pe.wait_ge(mx["al"], 6 * n + l - 1)
                        pe.wait_ge(mx["t"], 12 * n + 2 * l - 3)
                        for x in range(4):
                            last = pe.matmul(ps[:, 4, x * P:x * P + P], AL[:, x, :], TM[:, x, :], start=True, stop=True)
                        last.then_inc(mx["x"], 1)
                    else:
                        pe.wait_ge(mx["xc"], 6 * n + l - 1)
                        for x in range(4):
                            last = pe.matmul(ps[:, 5, x * P:x * P + P], XM[:, x, :], TT[:, x, :], start=True, stop=True)
                        if l < LEVELS:
                            for x in range(4):
                                last = pe.matmul(ps[:, 6, x * P:x * P + P], TT[:, x, :], XM[:, x, :],
                                                 start=True, stop=True)
                        last.then_inc(mx["p"], 1)
                if hp in (14, 16, 18, 20):
                    i = (hp - 14) // 2
                    pe.wait_ge(mx["us"], 6 * n + 5)
                    if i:
                        pe.wait_ge(mx["sn"], 16 * n + 4 * i)
                    for x in range(4):
                        last = pe.matmul(ps[:, 7, x * P:x * P + P],
                                         small[:, 3, 4 * i + x:4 * i + x + 1].broadcast_to([P, P]), ident,
                                         start=True, stop=True)
                    last.then_inc(mx["ub"], 1)
                if hp == 24:
                    pe.wait_ge(mx["t"], 12 * n + 12)
                    for j in range(2):
                        pe.matmul(ps[:, 4, j * P:j * P + P], TT[:, 2 * j, :], vb[:, 2 * j, :], start=True, stop=True)
                    for j in range(2):
                        last = pe.matmul(ps[:, 5, j * P:j * P + P], kbe[:, 2 * j + 1, :], TT[:, 2 * j + 1, :],
                                         start=True, stop=True)
                    last.then_inc(mx["u0"], 1)
                if hp == 25:
                    pe.wait_ge(mx["u0c"], 2 * n + 2)
                    for j in range(2):
                        last = pe.matmul(ps[:, 6, j * P:j * P + P], k_end[:, 2 * j, :], u[:, 2 * j, :],
                                         start=True, stop=True)
                    last.then_inc(mx["s1"], 1)
                if hp == 26:
                    pe.wait_ge(mx["s1c"], n + 1)
                    for j in range(2):
                        o = ps[:, 4, 256 + j * P:256 + j * P + P]
                        pe.matmul(o, TT[:, 2 * j + 1, :], vb[:, 2 * j + 1, :], start=True, stop=False)
                        last = pe.matmul(o, nwT[:, j, :], S[:, j, 0, :], start=False, stop=True)
                    last.then_inc(mx["u1"], 1)
                if hp == 27:
                    pe.wait_ge(mx["u1c"], n + 1)
                    for j in range(2):
                        pe.matmul(ps[:, 5, 256 + j * P:256 + j * P + P], k_end[:, 2 * j + 1, :], u[:, 2 * j + 1, :],
                                  start=True, stop=True)
                    for x in range(4):
                        o = ps[:, 6, x * P:x * P + P]
                        last = pe.matmul(o, u[:, x, :], QK[:, x, :], start=True, stop=(x % 2 == 0))
                        if x % 2:
                            last = pe.matmul(o, S[:, x // 2, 0, :], eb[:, x, :], start=False, stop=True)
                    last.then_inc(mx["so"], 1)
                if hp == 29:
                    out_sum(n)

            def out_sum(n):
                pe.wait_ge(mx["osq"], n + 1)
                pe.wait_ge(mx["s2"], 2 * n + 2)
                for j in range(2):
                    last = pe.matmul(ps[:, 4 + j, 0:T], ones[:, :], sq[:, j], start=True, stop=True)
                last.then_inc(mx["oss"], 1)

            def a_step(hp, n, k):
                if hp == 8:
                    pe.wait_ge(a_["wp"], 2 * k + 1)
                    pe.wait_ge(mx["ors"], n)
                    for x in range(4):
                        pe.transpose(ps[:, 6, x * P:x * P + P], kend_f[:, x, :], ident)
                    for x in range(4):
                        last = pe.transpose(ps[:, 7, x * P:x * P + P],
                                            qkv[:, 2, x // 2, (x % 2) * P:(x % 2) * P + P], ident)
                    last.then_inc(a_["tr"], 1)
                if hp in (10, 12, 14, 16):
                    i = (hp - 10) // 2
                    if i:
                        pe.wait_ge(mx["sn"], 16 * n + 4 * i)
                    else:
                        pe.wait_ge(a_["tm"], 2 * k + 2)
                    for x in range(4):
                        y = 4 * i + x
                        last = pe.matmul(ps[:, 7, x * P:x * P + P],
                                         v_s[:, y:y + 1].broadcast_to([P, P]), ident,
                                         start=True, stop=True)
                    last.then_inc(mx["ub"], 1)
                if hp in (16, 18, 20, 22):
                    x = (hp - 16) // 2
                    b0 = 4 + 2 * (x % 2)
                    if x == 0:
                        pe.wait_ge(a_["w"], 14 * k + 14)
                    if x == 1:
                        pe.wait_ge(mx["sn"], 16 * n + 16)
                    if x >= 2:
                        pe.wait_ge(a_["pr"], 8 * k + 2 * x - 2)
                    t = slice((x % 2) * P, (x % 2) * P + P)
                    pe.matmul(ps[:, b0, 0:P], nrm[:, 0, x // 2, t], qA[:, x // 2, t], start=True, stop=True)
                    for l in range(1, LEVELS + 1):
                        w = lev[:, l - 1, x * P:x * P + P]
                        last = pe.matmul(ps[:, b0 + l // 4, (l % 4) * P:(l % 4) * P + P], w, w, start=True, stop=True)
                    last.then_inc(a_["at"], 1)
                if hp == 24:
                    pe.wait_ge(a_["pr"], 8 * k + 6)
                    for x in range(16):
                        last = pe.matmul(ps[:, 4, 256 + x:257 + x], Ss[:, x, :], q_s[:, x:x + 1],
                                         start=True, stop=True)
                    last.then_inc(a_["vs"], 1)
                    for j in range(2):
                        last = pe.matmul(ps[:, 4, j * P:j * P + P], ke_tm[:, 2 * j, :], v_tm[:, 2 * j, :],
                                         start=True, stop=True)
                    last.then_inc(mx["s1"], 1)
                if hp == 26:
                    pe.wait_ge(mx["s1c"], n + 1)
                    pe.wait_ge(a_["rd"], 4 * k + 4)
                    pe.wait_ge(a_["wp"], 2 * k + 2)
                    for j in range(2):
                        pe.matmul(ps[:, 5, 256 + j * P:256 + j * P + P], ke_tm[:, 2 * j + 1, :], v_tm[:, 2 * j + 1, :],
                                  start=True, stop=True)
                    for x in range(4):
                        o = ps[:, 6, x * P:x * P + P]
                        last = pe.matmul(o, v_tm[:, x, :], attT[:, x, :], start=True, stop=(x % 2 == 0))
                        if x % 2:
                            last = pe.matmul(o, S[:, x // 2, 0, :], nwT[:, x // 2, :], start=False, stop=True)
                    last.then_inc(mx["so"], 1)
                if hp == 29:
                    out_sum(n)

            def round_(r, mixer):
                for pos in range(SLOTS):
                    q = pos // 4
                    if pos % 4 == 0:
                        bank_free(q % 2, 2 * r + q // 2)
                    for half in range(2):
                        chunk(SLOTS * r + pos, pos % 4, q % 2, 4 * (pos % 4), KT, act_hi, act_lo, half)
                        mixer(2 * pos + half)

            def mixer0(hp):
                if hp in (0, 2):
                    turn_input(2 + hp // 2)
                if hp in (1, 3, 5):
                    pe.wait_ge(xn_lo, 2 * hp + 6)
                if hp == 6:
                    turn_params()
                if hp == 7:
                    gate_columns()
                if hp == 9:
                    turn_gates()
                if hp == 15:
                    gating()
                if 18 <= hp < 30:
                    turn_x(hp - 18)

            pe.wait_ge(x_n, 3)
            turn_input(0)
            turn_input(1)
            pe.wait_ge(xn_lo, 4)
            round_(0, mixer0)
            pe.wait_ge(raw_cp, 12)
            round_(1, lambda hp: b_step(hp, 0))
            with pe.Fori(2, B_ROUNDS) as r:
                round_(r, lambda hp: b_step(hp, r - 1))
            round_(4, lambda hp: b_step(hp, 3))
            round_(5, lambda hp: a_step(hp, 4, 0))
            round_(6, lambda hp: a_step(hp, 5, 1))

            def gate_products(w):
                for t in range(4):
                    last = pe.matmul(ps[:, 4 + t, 0:T], wbd[:, w, t, :], qkv[:, t // 2, t % 2, :], start=True, stop=True)
                return last

            def product_sum(n):
                pe.wait_ge(o_acc, 7 * n + 7)
                for t in range(2):
                    last = pe.matmul(ps[:, 4, 0:T], ones[:, :], sacc[:, t], start=(t == 0), stop=(t == 1))
                last.then_inc(o_pe, 1)

            for s, (g, i) in enumerate(OUT_START):
                if i == 1:
                    bank_free(g, OUT_G0 // 2)
                if s == 4:
                    pe.wait_ge(mx["olo"], 6)
                if s == 6:
                    pe.wait_ge(c_["lo"], 1)
                chunk(OUT_C0 + s, s % RING, g, 4 * i, KT, cat_hi, cat_lo, begin=4)
                if s == 0:
                    pe.wait_ge(wbd_in, 64)
                    pe.wait_ge(silu_done, 28)
                    pe.wait_ge(mx["ors"], 6)
                    gate_products(0).then_inc(c_["r"], 1)
                if s == 1:
                    pe.wait_ge(c_["prei"], 4)
                    gate_products(1).then_inc(c_["i"], 1)
            pe.wait_ge(c_["h"], 5)
            tb, tc = tail_b[:, :, :].rearrange("p a k -> p (a k)"), tail_c[:, :, :].rearrange("p a k -> p (a k)")
            pe.transpose(ps[0:72, 6, 0:P], tb[:, 0:72], ident)
            pe.transpose(ps[0:120, 6, P:2 * P], tb[:, 72:192], ident)
            pe.transpose(ps[0:72, 6, 2 * P:3 * P], tb[:, 192:264], ident)
            pe.transpose(ps[0:80, 6, 3 * P:4 * P], tc[:, 0:80], ident).then_inc(tl_pe, 1)
            with pe.Fori(1, OUT_GROUPS // 2) as h:
                for n in range(2):
                    bank_free(n, h + OUT_G0 // 2)
                    for i in range(4):
                        chunk(8 * h + OUT_C0 + 4 * n + i, i, n, 4 * i, KT, cat_hi, cat_lo)
            product_sum(0)

            for n in range(2):
                bank_free(n, FF_G0 // 2)
                for i in range(4):
                    if n == 0:
                        pe.wait_ge(nz_lo, 1 + i)
                    chunk(FF_C0 + 4 * n + i, i, n, 4 * i, KT, act_hi, act_lo)
                    if (n, i) == (1, 1):
                        input_sum()
            with pe.Fori(1, FF_PAIRS) as g:
                for n in range(2):
                    bank_free(n, g + FF_G0 // 2)
                    for i in range(4):
                        chunk(8 * g + FF_C0 + 4 * n + i, i, n, 4 * i, KT, act_hi, act_lo)

            pe.wait_ge(nz_lo, 3 + FF_PAIRS)
            with pe.Fori(0, 2) as h:
                for g in range(DOWN_GROUPS // 2):
                    bank_free(g % 2, 2 * h + (DOWN_G0 + g) // 2)
                    for i in range(DOWN_CH):
                        c = DOWN_CH * g + i
                        if g == 0 and i == DOWN_CH - 1:
                            pe.wait_ge(nz_lo, 4 + FF_PAIRS)
                        chunk(44 * h + DOWN_C0 + c, c % RING, g % 2, CK * i, FT, hid_hi, hid_lo)
            product_sum(1)

            for i, q in enumerate(Y_ORDER):
                if i >= 2:
                    pe.wait_ge(y_cp, 3 * i - 3)
                for h in range(2):
                    if q == 3:
                        pe.wait_ge(o_pool, 4)
                    else:
                        pe.wait_ge(o_y, 2 + 2 * q + h + 1)
                    for t, n in enumerate((P, P, NB)):
                        for k in (2 * h, 2 * h + 1):
                            last = pe.transpose(ps[0:n, 3 * (i % 2) + t, k * P:k * P + P],
                                                ffg[:, 4 * q + k, t * P:t * P + n], ident)
                        if h == 1:
                            last.then_inc(y_pe, 1)

        @block.scalar
        def _(act):
            def A(out, in_, f=ACT.Copy, **kw):
                return act.activation(out, in_, f, **kw)

            def split(turn, slot, first=False):
                act.wait_ge(raw_in[slot], 16 * turn + 16)
                if not first:
                    act.wait_ge(pe_used, RING * turn + slot - RING + 1)
                A(w_hi[:, slot], raw[:, slot]).then_inc(hi_done, 1)

            def ln_exp_tables():
                act.preload_act_table_set("natural_log_exp_and_others")

            ln_exp_tables()
            for i, (t, n) in enumerate(((2, NB), (0, P), (1, P))):
                act.wait_ge(x_in[t], 16)
                A(xn[0:n, t], xtok[t][0:n, :], ACT.Square, accum_out=xss[0:n, 0, t:t + 1]).then_inc(x_ss, 1)
                if i == 0:
                    act.wait_ge(pool_c, 4)
                act.wait_ge(x_ss, 3 * i + 1)
                A(xss[0:n, 1, t:t + 1], xss[0:n, 0, t:t + 1], ACT.Ln, scale=1.0 / D, bias=eps[0:n]).then_inc(x_ss, 1)
                act.wait_ge(x_ss, 3 * i + 2)
                A(xss[0:n, 1, t:t + 1], xss[0:n, 1, t:t + 1], ACT.Exp, scale=-0.5).then_inc(x_ss, 1)
            act.wait_ge(gain_in, 1)
            for q in range(4):
                if q < AHEAD:
                    split(0, q, first=True)
                for k in range(4 * q, 4 * q + 4):
                    act.wait_ge(xn_pe, k + 1)
                    A(act_hi[:, k], ps[:, 2 + k % 4, 0:T], scale=params[:, G_MIX_PRE + k:G_MIX_PRE + k + 1])\
                        .then_inc(xn_hi, 1)
            act.wait_ge(gw_in, 16)
            A(gw_hi[:, :, :], gw[:, :, :]).then_inc(gw_s, 1)

            def rms():
                ln_exp_tables()
                act.wait_ge(nz_pe, 1)
                A(rbc[:, :], ps[:, 5, 0:T], ACT.Ln, scale=1.0 / D, bias=eps).then_inc(nz_r, 1)
                act.wait_ge(nz_r, 1)
                A(rbc[:, :], rbc[:, :], ACT.Exp, scale=-0.5).then_inc(nz_r, 1)

            def gating():
                act.wait_ge(st_dve, 10)
                A(zz[:, 1, :], zz[:, 0, :], ACT.Abs).then_inc(st_act, 1)
                act.wait_ge(st_act, 1)
                A(zz[:, 1, :], zz[:, 1, :], ACT.Exp, scale=-1.0).then_inc(st_act, 1)
                act.wait_ge(bc_in, 32)
                A(bcA[:, :], bcA[:, :], ACT.Exp).then_inc(st_act, 1)
                act.wait_ge(st_dve, 10)
                A(gt[:, :, 0:8], gt[:, :, 0:8], ACT.Sigmoid).then_inc(st_act, 1)

            def gating_table():
                act.wait_ge(st_pe, 4)
                A(gb[:, :, :], ps[:, 6, 64:96].rearrange("p (a b) -> p a b", a=2)).then_inc(st_act, 1)
                A(sgates[:, 0], ps[:, 6, 128:192].rearrange("p (k j) -> p k j", k=4), ACT.Exp).then_inc(st_act, 1)
                A(sgates[:, 1], ps[:, 6, 192:256].rearrange("p (k j) -> p k j", k=4)).then_inc(st_act, 1)
                act.wait_ge(st_act, 5)
                by_chunk = gb[:, :, :].rearrange("p a (c k j) -> p a c k j", c=2, k=4)
                for c in range(2):
                    gv = gates[:, :, :, c:4:2]
                    A(gv[:, F_EEND], by_chunk[:, 1, c], ACT.Exp).then_inc(st_act, 1)
                    A(gv[:, F_BETAEXP], by_chunk[:, 0, c], ACT.Exp).then_inc(st_act, 1)

            def gating_end():
                act.wait_ge(st_dve, 33)
                A(gates[:, F_KEND], gates[:, F_KEND], ACT.Exp).then_inc(st_act, 1)

            def acc_ready(g):
                act.wait_ge(pe_used, 4 * g + 4)

            def evac_conv(g, par, n, slot, tail, tile0):
                acc_ready(g)
                act.wait_ge(hist_in, 4 * n + 4)
                A(xraw[:, slot, :, 3:3 + L], acc(par)[:, :, 0:L]).then_inc(raw_q, 1)
                new = xraw[:, slot, :, 3 + L:XW].rearrange("p t (b j) -> p t b j", j=CONVW)[:, :, :, 3]
                A(new, acc(par)[:, :, L:T]).then_inc(raw_q, 1)
                A(tail[:, 0:11, ds(tile0, 2)], acc(par)[:, :, L - 3:T].rearrange("p t k -> p k t"))\
                    .then_inc(drained[par], 1)

            def silu_conv(n, which, f=ACT.Silu):
                act.wait_ge(conv_done, n + 1)
                A(qkv[:, which, :, 0:L], conv[:, :, 0:L], f).then_inc(silu_done, 1)
                A(qkv[:, which, :, L:T], conv[:, :, L + 3:CW:CONVW], f).then_inc(silu_done, 1)

            def evac_plain(g, par, which, f):
                acc_ready(g)
                A(qkv[:, which], acc(par), f).then_inc(drained[par], 1)

            def b_step(pos, n):
                first = isinstance(n, int) and n == 0
                if pos == 0:
                    act.wait_ge(silu_done, 6 * n + 6)
                    if not first:
                        act.wait_ge(mx["oss"], n)
                    A(sq[:, :, :], qkv[:, 0:2].rearrange("p a j t -> p (a j) t"), ACT.Square).then_inc(mx["sq"], 1)
                if pos == 1:
                    ln_exp_tables()
                    act.wait_ge(mx["ss"], n + 1)
                    if not first:
                        act.wait_ge(mx["og"], 2 * n)
                    A(rs[:, :, :], ps[:, 4:8, 0:T], ACT.Ln, bias=eps).then_inc(mx["ln"], 1)
                    act.wait_ge(mx["ln"], n + 1)
                    A(rs[:, :, :], rs[:, :, :], ACT.Exp, scale=-0.5).then_inc(mx["rs"], 1)
                if pos == 2:
                    act.wait_ge(mx["d"], 2 * n + 1)
                    A(eb[:, :, :], quad(4), ACT.Exp).then_inc(mx["eb"], 1)
                if pos == 3:
                    act.wait_ge(mx["d"], 2 * n + 2)
                    A(decay[:, :, :], decay[:, :, :], ACT.Exp).then_inc(mx["dec"], 1)
                if pos == 5:
                    act.wait_ge(mx["t1"], n + 1)
                    A(TM, quad(6)).then_inc(mx["t"], 1)
                if 6 <= pos <= 11:
                    l = pos - 4
                    act.wait_ge(mx["x"], 6 * n + l - 1)
                    A(XM, quad(4)).then_inc(mx["xc"], 1)
                if pos == 12:
                    act.wait_ge(mx["u0"], n + 1)
                    A(u[:, 0:4:2, :], quad(4)[:, 0:2]).then_inc(mx["u0c"], 1)
                    A(nwT[:, :, :], quad(5)[:, 0:2], scale=-1.0).then_inc(mx["u0c"], 1)
                    act.wait_ge(mx["s1"], n + 1)
                    A(S[:, :, 0, :], quad(6)[:, 0:2]).then_inc(mx["s1c"], 1)
                if pos == 13:
                    act.wait_ge(mx["u1"], n + 1)
                    A(u[:, 1:4:2, :], quad(4)[:, 2:4]).then_inc(mx["u1c"], 1)
                finish(pos, n)

            def finish(pos, n):
                if pos == 13:
                    act.wait_ge(mx["so"], n + 1)
                    A(oT[:, :, 0:L], ps[:, 6, :].rearrange("p (j t) -> p j t", j=2)).then_inc(mx["oc"], 1)
                if pos == 14:
                    act.wait_ge(mx["oc"], n + 1)
                    act.wait_ge(mx["os"], n + 1)
                    A(sq[:, 0:2], oT[:, :, :], ACT.Square).then_inc(mx["osq"], 1)
                if pos == 15:
                    ln_exp_tables()
                    act.wait_ge(mx["oss"], n + 1)
                    A(rs[:, 0:2], ps[:, 4:6, 0:T], ACT.Ln, scale=1.0 / P, bias=eps).then_inc(mx["oln"], 1)
                    act.wait_ge(mx["oln"], n + 1)
                    A(rs[:, 0:2], rs[:, 0:2], ACT.Exp, scale=-0.5).then_inc(mx["ors"], 1)

            def a_step(pos, n, k):
                if pos == 0:
                    act.wait_ge(drained[1], 2 * n + 1)
                    act.wait_ge(mx["so"], n)
                    ln_exp_tables()
                    A(nrm[:, 1], qkv[:, 1], ACT.Abs).then_inc(a_["ln"], 1)
                    act.wait_ge(a_["ln"], 3 * k + 1)
                    A(nrm[:, 1], nrm[:, 1], ACT.Exp, scale=-1.0).then_inc(a_["ln"], 1)
                    act.wait_ge(a_["ln"], 3 * k + 2)
                    A(nrm[:, 1], nrm[:, 1], ACT.Ln, bias=1.0).then_inc(a_["ln"], 1)
                if pos == 1:
                    act.wait_ge(a_["lf"], 2 * k + 1)
                    A(small[:, 0, :].rearrange("p (j b) -> p j b", j=2), nrm[:, 1, :, L:T], ACT.Exp).then_inc(a_["fs"], 1)
                    act.wait_ge(a_["lf"], 2 * k + 2)
                    A(nrm[:, 0], nrm[:, 0], ACT.Exp).then_inc(a_["k"], 1)
                if pos in (3, 5):
                    h = slice(0, 4) if pos == 3 else slice(4, 7)
                    act.wait_ge(a_["d"], 14 * k + (8 if pos == 3 else 14))
                    A(lev[:, h], lev[:, h], ACT.Exp).then_inc(a_["e"], 1)
                if pos == 2:
                    act.wait_ge(a_["b"], 4 * k + 4)
                    for x in range(4):
                        A(kend_f[:, x, :], bA[:, x, :], ACT.Exp, scale=-1.0, bias=bA[:, x, P - 1:P]).then_inc(a_["ex"], 1)
                    A(nwT[:, :, :], bA[:, 1:4:2, :], ACT.Exp).then_inc(a_["ex"], 1)
                    A(small[:, 1, 0:4], bA[:, :, P - 1], ACT.Exp).then_inc(a_["ex"], 1)
                if pos == 4:
                    act.wait_ge(a_["tr"], k + 1)
                    A(v_tm, quad(7)).then_inc(a_["tm"], 1)
                    A(ke_tm, quad(6)).then_inc(a_["tm"], 1)
                if pos == 12:
                    act.wait_ge(mx["s1"], n + 1)
                    A(S[:, :, 0, :], quad(4)[:, 0:2]).then_inc(mx["s1c"], 1)
                finish(pos, n)

            def round_(r, kind, prev, mixer):
                for pos in range(SLOTS):
                    slot, turn = (pos + AHEAD) % RING, (pos + AHEAD) // RING
                    split(4 * r + turn, slot, first=(isinstance(r, int) and r == 0 and pos + AHEAD < RING))
                    q = pos // 4
                    if pos in (4, 8, 12):
                        evac_group(r, kind, q - 1)
                    if prev and pos == 6:
                        act.wait_ge(drained[1], 2 * r)
                        A(qkv[:, 3], qkv[:, 3], ACT.Silu).then_inc(g_done, 1)
                    if kind == "a" and pos == 6:
                        act.wait_ge(drained[0], 2 * r + 1)
                        A(qkv[:, 0], qkv[:, 0], ACT.Silu).then_inc(g_done, 1)
                    if kind == "b" and pos in (6, 10, 14):
                        if not isinstance(r, int) or r > 0:
                            act.wait_ge(mx["nrm"], 2 * r)
                            if pos == 14:
                                act.wait_ge(mx["us"], 6 * r)
                        silu_conv(3 * r + q - 1, q - 1)
                    if kind == "c" and pos in (6, 10):
                        free_qkv(r, q - 1)
                        silu_conv(12 + q - 1, q - 1, ACT.Copy)
                    mixer(pos)
                    if prev and pos == 1:
                        if not isinstance(r, int) or r > 1:
                            act.wait_ge(mx["og"], 2 * r - 2)
                        evac_plain(4 * r - 1, 1, 3, ACT.Copy)

            def evac_group(r, kind, q):
                if kind == "b":
                    evac_conv(4 * r + q, q % 2, 3 * r + q, q % 2, tail_b, 2 * r + 8 * q)
                elif kind == "a":
                    free_qkv(r, q)
                    evac_plain(4 * r + q, q % 2, q, ACT.Copy)
                elif q < 2:
                    evac_conv(4 * r + q, q % 2, 12 + q, q % 2, tail_c, 2 * q)
                else:
                    free_qkv(r, q)
                    evac_plain(4 * r + q, q % 2, q, ACT.Gelu_apprx_tanh)

            def free_qkv(r, q):
                n = r - 1
                if n < B_ROUNDS:
                    act.wait_ge(mx["nrm"], 2 * n + 2)
                    if q == 2:
                        act.wait_ge(mx["us"], 6 * n + 6)
                elif q == 0:
                    act.wait_ge(a_["q"], 3 * (n - B_ROUNDS) + 3)
                elif q == 1:
                    act.wait_ge(a_["lf"], 2 * (n - B_ROUNDS) + 2)
                else:
                    act.wait_ge(a_["tr"], n - B_ROUNDS + 1)

            def mixer0(pos):
                if pos == 5:
                    gating()
                if pos == 9:
                    gating_table()
                if pos == 10:
                    gating_end()

            round_(0, "b", False, mixer0)
            round_(1, "b", True, lambda pos: b_step(pos, 0))
            with act.Fori(2, B_ROUNDS) as r:
                round_(r, "b", True, lambda pos: b_step(pos, r - 1))
            round_(4, "a", True, lambda pos: b_step(pos, 3))
            round_(5, "a", True, lambda pos: a_step(pos, 4, 0))
            round_(6, "c", True, lambda pos: a_step(pos, 5, 1))

            def out_evac(k, par, n, c_ready, gain, dst):
                act.wait_ge(pe_used, c_ready)
                if k >= 3:
                    act.wait_ge(o_acc, 7 * n + k - 2)
                elif n:
                    act.wait_ge(o_acc, 7)
                    act.wait_ge(o_pe, 1)
                elif k == 0:
                    act.wait_ge(mx["st"], 64 * (ROUNDS - 1))
                A(sqo[:, k % 2] if k else sacc[:, :, :], acc(par), ACT.Square).then_inc(o_sq, 1)
                for t in range(2):
                    tile = 2 * k + t
                    last = A(dst[:, tile], ps[:, 2 * par + t, 0:T], scale=params[:, gain + tile:gain + tile + 1])
                    if t == 1:
                        last.then_inc(drained[par], 1)

            def rg_step(pos):
                if pos == 0:
                    act.wait_ge(mx["og"], 12)
                    evac_plain(27, 1, 3, ACT.Gelu_apprx_tanh)
                if pos == 1:
                    act.wait_ge(c_["r"], 1)
                    for t in range(4):
                        A(nrm[:, t // 2, t % 2], ps[:, 4 + t, 0:T], ACT.Sigmoid,
                          bias=params[:, C_BA + t:C_BA + t + 1]).then_inc(c_["prei"], 1)
                    act.wait_ge(c_["prei"], 4)
                    act.wait_ge(st_dve, 34)
                    for t in range(4):
                        A(ca[:, t], nrm[:, t // 2, t % 2], ACT.Exp, scale=lamc[:, 0, t:t + 1]).then_inc(c_["a"], 1)
                    for t in range(4):
                        A(cth[:, t], nrm[:, t // 2, t % 2], ACT.Tanh, scale=lamc[:, 1, t:t + 1]).then_inc(c_["a"], 1)
                if pos == 2:
                    act.wait_ge(c_["i"], 1)
                    for t in range(4):
                        A(rs[:, t], ps[:, 4 + t, 0:T], ACT.Sigmoid,
                          bias=params[:, C_BX + t:C_BX + t + 1]).then_inc(c_["prei"], 1)
                if pos == 3:
                    act.wait_ge(c_["x"], 2)
                    A(cm[:, :, :], cm[:, :, :], ACT.Sqrt).then_inc(c_["a"], 1)

            for pos in range(4 * OUT_GROUPS):
                slot = (pos + AHEAD) % RING
                split((OUT_C0 + pos + AHEAD) // RING, slot)
                rg_step(pos)
                if pos == 7:
                    out_evac(0, 0, 0, OUT_C0 + 7, G_MIX_POST, mixg)
                elif pos > 7 and pos % 4 == 0:
                    g = pos // 4 - 1
                    out_evac(g, g % 2, 0, OUT_C0 + 4 * g + 4, G_MIX_POST, mixg)
            g = OUT_GROUPS - 1
            ln_exp_tables()
            out_evac(g, g % 2, 0, OUT_C0 + 4 * g + 4, G_MIX_POST, mixg)

            def out_norm(n, bank):
                act.wait_ge(o_pe, n + 1)
                A(rbc[:, :], ps[:, bank, 0:T], ACT.Ln, scale=1.0 / D, bias=eps).then_inc(o_r, 1)
                act.wait_ge(o_r, 2 * n + 1)
                A(rbc[:, :], rbc[:, :], ACT.Exp, scale=-0.5).then_inc(o_r, 1)

            out_norm(0, 4)
            for q in range(4):
                if 1 <= q < 3:
                    act.wait_ge(o_y, q)
                if q == 3:
                    act.wait_ge(o_pool, 2)
                for k in range(4 * q, 4 * q + 4):
                    if k in (0, 2):
                        act.wait_ge(o_h, k + 2)
                    last = A(act_hi[:, k], xT[:, k], scale=params[:, G_FFN_PRE + k:G_FFN_PRE + k + 1])
                last.then_inc(nz_hi, 1)

            def gate_silu(g):
                act.wait_ge(drained[0], g + FF_G0 // 2 + 1)
                A(sgate[:, :, :], sgate[:, :, :], ACT.Silu).then_inc(gate_act, 1)

            def hid_split(g):
                act.wait_ge(drained[1], g + FF_G0 // 2 + 1)
                act.wait_ge(tl_out, 16 * 20)
                A(hid_hi[:, ds(2 * g, 2)], hidF[:, :, :]).then_inc(ff_hi, 1)

            for i in range(8):
                slot, turn = (i + AHEAD) % RING, (i + AHEAD) // RING
                split(FF_C0 // RING + turn, slot)
                if i < 4:
                    A(hF[:, 4 * i:4 * i + 4], xT[:, 4 * i:4 * i + 4], ACT.Square).then_inc(nz_sq, 1)
                if i == 6:
                    act.wait_ge(o_y, 2)
                    act.wait_ge(o_pool, 2)
                    rms()
                if i == 7:
                    gate_silu(0)
            with act.Fori(1, FF_PAIRS) as g:
                for i in range(8):
                    slot, turn = (i + AHEAD) % RING, (i + AHEAD) // RING
                    split(2 * g + FF_C0 // RING + turn, slot)
                    if i == 1:
                        hid_split(g - 1)
                    if i == 5:
                        gate_silu(g)
            for g in range(DOWN_GROUPS):
                for i in range(DOWN_CH):
                    c = DOWN_CH * g + i + AHEAD
                    if DOWN_C0 + c < CHUNKS:
                        split((DOWN_C0 + c) // RING, c % RING)
                    if g == 0 and i == 1:
                        hid_split(FF_PAIRS - 1)
                    if i == 0 and g:
                        out_evac(g - 1, (g - 1) % 2, 1, DOWN_C0 + DOWN_CH * g, G_FFN_POST, ffg)
            g = DOWN_GROUPS
            ln_exp_tables()
            out_evac(g - 1, (g - 1) % 2, 1, DOWN_C0 + DOWN_CH * g, G_FFN_POST, ffg)
            out_norm(1, 4)
            for i, q in enumerate(Y_ORDER):
                for t, n in enumerate((P, P, NB)):
                    act.wait_ge(y_pe, 3 * i + t + 1)
                    A(ytok[0:n, t, 512 * q:512 * q + 512], ps[0:n, 3 * (i % 2) + t, :]).then_inc(y_cp, 1)

        @block.vector
        def _(dve):
            mul, add, sub = ALU.mult, ALU.add, ALU.subtract
            tt, stt, tsc = dve.tensor_tensor, dve.scalar_tensor_tensor, dve.tensor_scalar

            def lo(c, slot):
                dve.wait_ge(hi_done, c + 1)
                tt(w_lo[:, slot], raw[:, slot], w_hi[:, slot].bitcast(F32), sub).then_inc(lo_done, 1)

            for i, (t, n) in enumerate(((2, NB), (0, P), (1, P))):
                dve.wait_ge(x_ss, 3 * i + 3)
                tsc(xn[0:n, t], xtok[t][0:n, :], xss[0:n, 1, t:t + 1], None, mul).then_inc(x_n, 1)
                if i == 0:
                    dve.wait_ge(par0_pe, 1)
                    dve.tensor_copy(params[:, 0:112], ps[:, 6, 0:112]).then_inc(gain_in, 1)
            dve.wait_ge(gain_in, 1)
            for q in range(4):
                if q < AHEAD:
                    lo(q, q)
                for k in range(4 * q, 4 * q + 4):
                    dve.wait_ge(xn_hi, k + 1)
                    stt(act_lo[:, k], ps[:, 2 + k % 4, 0:T], params[:, G_MIX_PRE + k:G_MIX_PRE + k + 1],
                        act_hi[:, k].bitcast(F32), mul, sub).then_inc(xn_lo, 1)
            dve.wait_ge(gw_s, 1)
            tt(gw_lo[:, :, :], gw[:, :, :], gw_hi[:, :, :].bitcast(F32), sub).then_inc(gw_s, 1)

            def parameters():
                dve.wait_ge(st_pe, 1)
                dve.tensor_copy(params[:, 112:PCOLS], ps[:, 6, 112:PCOLS]).then_inc(st_dve, 1)
                hv = hist_b[:, :, :, :].rearrange("p b j k -> p (b j k)")
                dve.tensor_copy(hv[:, 0:512], ps[:, 7, :]).then_inc(st_dve, 1)
                dve.tensor_copy(hv[:, 512:576], ps[:, 4, 0:64]).then_inc(st_dve, 1)
                for i in range(3):
                    dve.memset(small[:, i, :], 0.0).then_inc(st_dve, 1)
                dve.wait_ge(st_dve, 3)

            def residual_copy(q):
                t, k0 = q // 4, 4 * (q % 4)
                n = P if t < 2 else NB
                dve.wait_ge(raw_pe, q + 1)
                dve.tensor_copy(xT[:, k0:k0 + 4, t * P:t * P + n], quad(TURN_BANKS[q % 3])[:, :, 0:n])\
                    .then_inc(raw_cp, 1)

            def gating():
                dve.wait_ge(st_pe, 3)
                dve.wait_ge(pool_c, 8)
                dve.tensor_copy(gt[:, 0:2, :], ps[:, 6, 0:32].rearrange("p (a b) -> p a b", a=2)).then_inc(st_dve, 1)
                dve.tensor_copy(gt[0:NB, 2, :], ps[0:NB, 6, 32:48]).then_inc(st_dve, 1)
                dve.wait_ge(st_dve, 9)
                dve.wait_ge(bc_in, 32)
                z = zz[:, 0, 0:24].rearrange("p (a b) -> p a b", a=3)
                tt(z, gt[:, :, 8:16], bcD[:, :].unsqueeze(1).broadcast_to([P, 3, 8]), add)
                tsc(zz[:, 0, 24:28], params[:, C_LAM:C_LAM + 4], -1.0, None, mul).then_inc(st_dve, 1)
                dve.wait_ge(st_act, 2)
                n = [10]

                def link(ins):
                    ins.then_inc(st_dve, 1)
                    n[0] += 1
                    dve.wait_ge(st_dve, n[0])

                link(tsc(zz[:, 2, :], zz[:, 1, :], 2.0, None, add))
                link(dve.reciprocal(zz[:, 2, :], zz[:, 2, :]))
                link(tt(zz[:, 2, :], zz[:, 2, :], zz[:, 1, :], mul))
                link(tt(zz[:, 3, :], zz[:, 2, :], zz[:, 2, :], mul))
                link(tsc(zz[:, 4, :], zz[:, 3, :], SERIES[0], None, mul))
                for c in SERIES[1:-1]:
                    link(stt(zz[:, 4, :], zz[:, 4, :], c, zz[:, 3, :], add, mul))
                link(stt(zz[:, 4, :], zz[:, 4, :], 1.0, zz[:, 2, :], add, mul))
                link(tsc(zz[:, 5, :], zz[:, 0, :], 0.0, None, ALU.max))
                link(stt(zz[:, 4, :], zz[:, 4, :], 2.0, zz[:, 5, :], mul, add))
                link(tsc(lamc[:, 1, :], zz[:, 4, 24:28], 8.0, None, mul))
                link(tsc(lamc[:, 0, :], zz[:, 4, 24:28], -8.0, None, mul))
                dve.wait_ge(st_act, 4)
                sp_ = zz[:, 4, 0:24].rearrange("p (a b) -> p a b", a=3)
                link(stt(gt[:, :, 8:16], sp_, -1.0, bcA[:, :].unsqueeze(1).broadcast_to([P, 3, 8]), mul, mul))
                for i, c0 in enumerate((8, 0)):
                    link(tt(sel[:, i], gt[0:8, 2, c0:c0 + 8].unsqueeze(2).broadcast_to([8, 8, 8]),
                            ident[0:8, 0:8].unsqueeze(1).broadcast_to([8, 8, 8]), mul))
                assert n[0] == 28 + 1, n[0]
                gtv = gt[:, 0:2, :].rearrange("p c (f k j) -> p c f k j", f=2, k=4)
                for c in range(2):
                    gv = gates[:, :, :, c:4:2]
                    dve.tensor_copy(gv[:, F_BETA], gtv[:, c, 0])
                    link(dve.tensor_copy(gv[:, F_G], gtv[:, c, 1]))

            def gating_table():
                dve.wait_ge(st_act, 11)
                gbv = gb[:, :, :].rearrange("p a (c k j) -> p a c k j", c=2, k=4)
                for c in range(2):
                    gv = gates[:, :, :, c:4:2]
                    dve.tensor_copy(gv[:, F_B], gbv[:, 0, c])
                    tt(gv[:, F_KEND], gbv[:, 1, c], gbv[:, 0, c], sub).then_inc(st_dve, 1)
                tt(gates[:, F_BETAEXP], gates[:, F_BETAEXP], gates[:, F_BETA], mul).then_inc(st_dve, 1)

            chain = sem("dve_chain")
            chained = [0]

            def link(ins, base=0):
                ins.then_inc(chain, 1)
                chained[0] += 1
                dve.wait_ge(chain, base + chained[0])

            def after(s, n):
                if not isinstance(n, int) or n > 0:
                    dve.wait_ge(s, n)

            def convolve(n, slot, base, bias=None):
                dve.wait_ge(raw_q, 2 * n + 2)
                after(silu_done, 2 * n)
                for j in range(CONVW):
                    for t in range(2):
                        w = convw[:, slot, t, j:j + 1]
                        x = xraw[:, slot, t, j:j + CW]
                        if j == 0 and bias is not None:
                            ins = tsc(conv[:, t], x, w, bias[:, t:t + 1], mul, add)
                        elif j == 0:
                            ins = tsc(conv[:, t], x, w, None, mul)
                        else:
                            ins = stt(conv[:, t], x, w, conv[:, t], mul, add)
                    if j < CONVW - 1:
                        link(ins, base)
                    else:
                        ins.then_inc(conv_done, 1)

            def b_step(pos, n):
                up4 = lambda f: pair[:, f, :].unsqueeze(2).broadcast_to([P, 4, P])
                if pos == 0:
                    after(mx["so"], n)
                    dve.tensor_copy(pair[:, :, :], gates[:, :, ds(n, 1), :].rearrange("p f o x -> p f (o x)"))\
                        .then_inc(mx["pair"], 1)
                    dve.tensor_copy(spair[:, :, :], sgates[:, :, ds(n, 1), :].rearrange("p f o x -> p f (o x)"))\
                        .then_inc(mx["pair"], 1)
                if pos == 1:
                    dve.wait_ge(mx["rs"], n + 1)
                    rv = rs[:, :, :].rearrange("p (a j) t -> p a j t", a=2)
                    stt(nrm[:, 0], qkv[:, 0], float(P) ** -0.5, rv[:, 0], mul, mul).then_inc(mx["nrm"], 1)
                    tt(nrm[:, 1], qkv[:, 1], rv[:, 1], mul).then_inc(mx["nrm"], 1)
                if pos == 2:
                    dve.wait_ge(mx["bc"], n + 1)
                    dve.wait_ge(mx["pair"], 2 * n + 2)
                    dve.wait_ge(mx["nrm"], 2 * n + 2)
                    tt(decay[:, :, :], quad(4), up4(F_B), sub).then_inc(mx["d"], 1)
                    dve.wait_ge(mx["d"], 2 * n + 1)
                    tsc(decay[:, :, :], decay[:, :, :], 0.0, None, ALU.min).then_inc(mx["d"], 1)
                    kn = nrm[:, 1, :, 0:L]
                    tt(kb[:, :, :].rearrange("p (j c) t -> p j (c t)", j=2), kn,
                       ps[:, 5, :].rearrange("p (j t) -> p j t", j=2), mul).then_inc(mx["kb"], 1)
                    tt(vb[:, :, :], quad(7), up4(F_BETA), mul).then_inc(mx["tm"], 1)
                    dve.wait_ge(mx["tr"], n + 1)
                    tt(k_end[:, :, :], quad(6), up4(F_KEND), mul).then_inc(mx["tm"], 1)
                    tt(kbe[:, :, :], quad(6), up4(F_BETAEXP), mul).then_inc(mx["tm"], 1)
                if pos == 3:
                    dve.wait_ge(mx["eb"], n + 1)
                    tt(eb[:, :, :].rearrange("p (j c) t -> p j (c t)", j=2), nrm[:, 0, :, 0:L],
                       eb[:, :, :].rearrange("p (j c) t -> p j (c t)", j=2), mul).then_inc(mx["qe"], 1)
                    tt(small[:, 0, :].rearrange("p (j b) -> p j b", j=2), nrm[:, 0, :, L:T], nrm[:, 1, :, L:T], mul)\
                        .then_inc(mx["qkp"], 1)
                if pos == 4:
                    dve.wait_ge(mx["g"], n + 1)
                    dve.wait_ge(mx["cau"], n + 1)
                    tt(AT[:, :, :], quad(4), decay[:, :, :], mul).then_inc(mx["at"], 1)
                    dve.wait_ge(mx["at"], 2 * n + 1)
                    m1 = masks[:, 1, :].unsqueeze(1).broadcast_to([P, 4, P])
                    tt(AL, AT[:, :, :], m1, mul).then_inc(mx["qe"], 1)
                    dve.wait_ge(mx["qe"], 2 * n + 2)
                    tt(TT[:, :, :], ident.unsqueeze(1).broadcast_to([P, 4, P]), AL, sub).then_inc(mx["tt"], 1)
                    tt(QK[:, :, :], quad(5), decay[:, :, :], mul).then_inc(mx["at"], 1)
                if pos == 5:
                    dve.wait_ge(mx["ks"], n + 1)
                    dve.wait_ge(mx["qk"], n + 1)
                    kq = ps[:, 7, 0:32].rearrange("p (x two) -> p x two", two=2)
                    n5 = 6 * n
                    tt(small[:, 2, :], kq[:, :, 1], spair[:, 0, :], mul).then_inc(mx["us"], 1)
                    tt(small[:, 4, :], kq[:, :, 0], spair[:, 0, :], mul).then_inc(mx["us"], 1)
                    dve.tensor_copy(small[:, 5, :], ps[:, 7, 32:48]).then_inc(mx["us"], 1)
                    dve.wait_ge(mx["us"], n5 + 1)
                    v_s = qkv[:, 2, :, L:T]
                    j2 = lambda a: a.rearrange("p (j b) -> p j b", j=2)
                    tt(j2(small[:, 2, :]), v_s, j2(small[:, 2, :]), sub).then_inc(mx["us"], 1)
                    dve.wait_ge(mx["us"], n5 + 4)
                    tt(small[:, 3, :], small[:, 2, :], spair[:, 1, :], mul).then_inc(mx["us"], 1)
                    dve.wait_ge(mx["us"], n5 + 5)
                    tt(small[:, 5, :], small[:, 5, :], small[:, 3, :], mul).then_inc(mx["us"], 1)
                    dve.wait_ge(mx["us"], n5 + 6)
                    tt(oT[:, :, L:T], j2(small[:, 4, :]), j2(small[:, 5, :]), add).then_inc(mx["os"], 1)
                if 6 <= pos <= 11:
                    l = pos - 4
                    dve.wait_ge(mx["p"], 6 * n + l - 1)
                    if l < LEVELS:
                        tt(TM, TM, quad(6), sub).then_inc(mx["t"], 1)
                    tt(TT[:, :, :], TT[:, :, :], quad(5), sub).then_inc(mx["t"], 1)
                if 7 <= pos <= 10:
                    state_update(n, pos - 7, nrm[:, 1])
                if pos == 13:
                    dve.wait_ge(mx["so"], n + 1)
                    dve.wait_ge(mx["s1c"], n + 1)
                    after(mx["st"], 64 * n)
                    for j in range(2):
                        stt(S[:, j, 1, :], S[:, j, 0, :], pair[:, F_EEND, 2 * j + 1:2 * j + 2],
                            quad(5)[:, 2 + j], mul, add).then_inc(mx["s2"], 1)

            def state_update(n, i, k_f):
                if i == 0:
                    dve.wait_ge(mx["sdec"], n + 1)
                dve.wait_ge(mx["ub"], 4 * n + i + 1)
                for x in range(4 * i, 4 * i + 4):
                    stt(Ss[:, x, :], ps[:, 7, (x % 4) * P:(x % 4) * P + P],
                        k_f[:, x // 8, L + x % 8:L + x % 8 + 1], Ss[:, x, :], mul, add).then_inc(mx["sn"], 1)

            def finish(n, tile0, gain):
                dve.wait_ge(mx["ors"], n + 1)
                stt(oT[:, :, :], oT[:, :, :], params[:, gain:gain + 1], rs[:, 0:2], mul, mul).then_inc(mx["og"], 1)
                dve.wait_ge(mx["og"], 2 * n + 1)
                tt(oT[:, :, :], oT[:, :, :], qkv[:, 3], mul).then_inc(mx["og"], 1)
                dve.wait_ge(mx["og"], 2 * n + 2)
                dve.tensor_copy(cat_hi[:, ds(tile0, 2)], oT[:, :, :]).then_inc(mx["ohi"], 1)
                dve.wait_ge(mx["ohi"], n + 1)
                tt(cat_lo[:, ds(tile0, 2)], oT[:, :, :], cat_hi[:, ds(tile0, 2)].bitcast(F32), sub)\
                    .then_inc(mx["olo"], 1)

            def a_step(pos, n, k):
                if pos == 0:
                    dve.wait_ge(mx["so"], n)
                    dve.wait_ge(a_["ln"], 3 * k + 3)
                    dve.tensor_copy(qA, qkv[:, 0, :, 0:L]).then_inc(a_["q"], 1)
                    dve.tensor_copy(q_s.rearrange("p (j b) -> p j b", j=2), qkv[:, 0, :, L:T]).then_inc(a_["q"], 1)
                    dve.tensor_copy(v_s.rearrange("p (j b) -> p j b", j=2), qkv[:, 2, :, L:T]).then_inc(a_["q"], 1)
                    stt(nrm[:, 1], qkv[:, 1], 0.0, nrm[:, 1], ALU.min, sub).then_inc(a_["lf"], 1)
                    dve.wait_ge(a_["lf"], 2 * k + 1)
                    tt(nrm[:, 0], nrm[:, 1], qkv[:, 1], sub).then_inc(a_["lf"], 1)
                    for x in range(4):
                        dve.tensor_tensor_scan(bA[:, x, :], ones[:, :], nrm[:, 1, x // 2, (x % 2) * P:(x % 2) * P + P],
                                               0.0, mul, add).then_inc(a_["b"], 1)
                if pos in (1, 2, 3):
                    dve.wait_ge(a_["b"], 4 * k + 4)
                    for l in ((0, 1, 2), (3, 4), (5, 6))[pos - 1]:
                        m = 1 << l
                        v = lambda a: a.rearrange("p (n h m) -> p n h m", h=2, m=m)
                        bv = v(sqv[:, 0:512])
                        mid = bv[:, :, 0, m - 1:m].broadcast_to([P, 256 // m, m])
                        tt(v(lev[:, l])[:, :, 0], mid, bv[:, :, 0], sub).then_inc(a_["d"], 1)
                        tt(v(lev[:, l])[:, :, 1], bv[:, :, 1], mid, sub).then_inc(a_["d"], 1)
                if 5 <= pos <= 8:
                    state_update(n, pos - 5, nrm[:, 0])
                if pos in (4, 5, 6, 7):
                    dve.wait_ge(a_["e"], 2 * k + (1 if pos < 6 else 2))
                    dve.wait_ge(a_["k"], k + 1)
                    dve.wait_ge(a_["q"], 3 * k + 3)
                    for l in ((0,), (1, 2), (3, 4), (5, 6))[pos - 4]:
                        m = 1 << l
                        h = lambda a: a.rearrange("p (n h m) -> p n h m", h=2, m=m)
                        for half, src in ((0, nrm[:, 0]), (1, qA)):
                            for_j = lev[:, l].rearrange("p (j n h m) -> p j n h m", j=2, h=2, m=m)[:, :, :, half]
                            sv = src[:, :, 0:L].rearrange("p j (n h m) -> p j n h m", h=2, m=m)[:, :, :, half]
                            tt(for_j, for_j, sv, mul).then_inc(a_["w"], 1)
                if pos == 12:
                    dve.wait_ge(a_["vs"], k + 1)
                    dve.wait_ge(mx["s1c"], n + 1)
                    dve.tensor_copy(oT[:, :, L:T], ps[:, 4, 256:272].rearrange("p (j b) -> p j b", j=2))\
                        .then_inc(mx["os"], 1)
                if pos in (8, 9, 10, 11):
                    x = pos - 8
                    b0 = 4 + 2 * (x % 2)
                    dve.wait_ge(a_["at"], 4 * k + x + 1)
                    if x:
                        dve.wait_ge(a_["rd"], 4 * k + x)
                    for h in range(2):
                        tt(prod[:, 4 * h:4 * h + 4], quad(b0 + h), masks[:, 4 * h:4 * h + 4, :], mul)\
                            .then_inc(a_["pr"], 1)
                    dve.wait_ge(a_["pr"], 8 * k + 2 * x + 2)
                    dve.tensor_reduce(attT[:, x, :], prod.rearrange("p l t -> p t l"), AX.X, ALU.add)\
                        .then_inc(a_["rd"], 1)
                if pos == 13:
                    dve.wait_ge(mx["so"], n + 1)
                    dve.wait_ge(mx["st"], 64 * n)
                    for j in range(2):
                        stt(S[:, j, 1, :], S[:, j, 0, :], small[:, 1, 2 * j + 1:2 * j + 2], quad(5)[:, 2 + j],
                            mul, add).then_inc(mx["s2"], 1)

            CV = 3

            def round_(r, kind, mixer, fin, before=lambda pos: None):
                for pos in range(SLOTS):
                    lo(SLOTS * r + pos + AHEAD, (pos + AHEAD) % RING)
                    q = pos // 4
                    before(pos)
                    if kind == "b" and pos in (4, 8, 12):
                        chained[0] = CV * (q - 1)
                        convolve(3 * r + q - 1, (q - 1) % 2, 3 * CV * r)
                    if kind == "c" and pos in (4, 8):
                        chained[0] = CV * (q - 1)
                        convolve(12 + q - 1, (q - 1) % 2, 12 * CV, params[:, C_BIAS + 2 * (q - 1):C_BIAS + 2 * q])
                    mixer(pos)
                    if pos == 15 and fin is not None:
                        finish(*fin)

            def mixer0(pos):
                if pos == 3:
                    parameters()
                if pos == 4:
                    dve.wait_ge(st_pe, 2)
                    dve.tensor_copy(bab[:, :], ps[0:16, 7, 0:T]).then_inc(st_dve, 1)
                if pos == 5:
                    gating()
                if pos == 9:
                    gating_table()

            def copies0(pos):
                if pos >= 10:
                    residual_copy(2 * pos - 20)
                    residual_copy(2 * pos - 19)

            round_(0, "b", mixer0, None, copies0)
            dve.wait_ge(st_act, 12)
            dve.wait_ge(st_dve, 34)
            round_(1, "b", lambda pos: b_step(pos, 0), (0, 4, B_NORM))
            with dve.Fori(2, B_ROUNDS) as r:
                round_(r, "b", lambda pos: b_step(pos, r - 1), (r - 1, 2 * r + 2, B_NORM))
            round_(4, "a", lambda pos: b_step(pos, 3), (3, 10, B_NORM))
            round_(5, "a", lambda pos: a_step(pos, 4, 0), (4, 0, A_NORM))
            round_(6, "c", lambda pos: a_step(pos, 5, 1), (5, 2, A_NORM))

            def add_squares(n, k):
                dve.wait_ge(o_sq, 8 * n + k + 1)
                if k > 1:
                    dve.wait_ge(o_acc, 7 * n + k - 1)
                tt(sacc[:, :, :], sacc[:, :, :], sqo[:, k % 2], add).then_inc(o_acc, 1)

            def rg_step(pos):
                if pos == 1:
                    dve.wait_ge(c_["a"], 4)
                    tt(cm[:, :, :], ca[:, :, :], ca[:, :, :], mul).then_inc(c_["x"], 1)
                    dve.wait_ge(c_["x"], 1)
                    dve.wait_ge(c_["a"], 8)
                    stt(cm[:, :, :], cm[:, :, :], 1.0, cth[:, :, :], add, mul).then_inc(c_["x"], 1)
                if pos == 3:
                    dve.wait_ge(c_["a"], 9)
                    dve.memset(cm[:, :, 0:1], 1.0).then_inc(c_["x"], 1)
                    dve.wait_ge(c_["x"], 3)
                    dve.wait_ge(c_["ix"], 1)
                    tt(cm[:, :, :], cm[:, :, :], rs[:, :, :], mul).then_inc(c_["x"], 1)
                    dve.wait_ge(c_["x"], 4)
                    for t in range(4):
                        last = dve.tensor_tensor_scan(sq[:, t, 0:L], ca[:, t, 0:L], cm[:, t, 0:L], 0.0, mul, add)
                    last.then_inc(c_["h"], 1)
                    h0 = params[:, RG_H:RG_H + 32].rearrange("p (b k) -> p k b", k=4)
                    tt(sq[:, :, L:T], ca[:, :, L:T], h0, mul).then_inc(c_["h"], 1)
                    dve.wait_ge(c_["h"], 2)
                    tt(sq[:, :, L:T], sq[:, :, L:T], cm[:, :, L:T], add).then_inc(c_["h"], 1)
                    dve.wait_ge(c_["h"], 3)
                    dve.wait_ge(drained[1], 14)
                    tt(cm[:, :, :], sq[:, :, :], qkv[:, 2:4].rearrange("p a j t -> p (a j) t"), mul).then_inc(c_["h"], 1)
                    dve.wait_ge(c_["h"], 4)
                    dve.tensor_copy(cat_hi[:, 12:16], cm[:, :, :]).then_inc(c_["hi"], 1)
                    dve.wait_ge(c_["hi"], 1)
                    tt(cat_lo[:, 12:16], cm[:, :, :], cat_hi[:, 12:16].bitcast(F32), sub).then_inc(c_["lo"], 1)
                if pos == 6:
                    dve.tensor_copy(tail_c[:, 11:20, :], sq[:, :, L - 1:T].rearrange("p k t -> p t k"))\
                        .then_inc(c_["h"], 1)

            for pos in range(4 * OUT_GROUPS):
                lo(OUT_C0 + pos + AHEAD, (pos + AHEAD) % RING)
                rg_step(pos)
                if pos > 8 and pos % 4 == 1:
                    add_squares(0, pos // 4 - 1)
                if pos == 13:
                    dve.wait_ge(tl_pe, 1)
                    for i, n in enumerate((72, 120, 72, 80)):
                        dve.tensor_copy(rows[0:n, i, :], ps[0:n, 6, i * P:i * P + P]).then_inc(tl_cp, 1)

            def scale_quarter(q, src):
                s = slice(4 * q, 4 * q + 4)
                tt(src[:, s], src[:, s], rbc[:, :].unsqueeze(1).broadcast_to([P, 4, T]), mul).then_inc(o_g, 1)

            def add_quarter(q, src, dst):
                dve.wait_ge(o_g, q)
                s = slice(4 * q, 4 * q + 4)
                tt(dst[:, s], xT[:, s], src[:, s], add).then_inc(o_y, 1)

            def input_lo(q):
                dve.wait_ge(nz_hi, 1 + q)
                for k in range(4 * q, 4 * q + 4):
                    last = stt(act_lo[:, k], xT[:, k], params[:, G_FFN_PRE + k:G_FFN_PRE + k + 1],
                               act_hi[:, k].bitcast(F32), mul, sub)
                last.then_inc(nz_lo, 1)

            add_squares(0, OUT_GROUPS - 1)
            dve.wait_ge(o_r, 2)
            dve.wait_ge(drained[1], 18)
            for t in (0, 2):
                h = slice(t, t + 2)
                tt(mixg[:, h], mixg[:, h], rbc[:, :].unsqueeze(1).broadcast_to([P, 2, T]), mul).then_inc(o_h, 1)
                dve.wait_ge(o_h, t + 1)
                tt(xT[:, h], xT[:, h], mixg[:, h], add).then_inc(o_h, 1)
            scale_quarter(1, mixg)
            input_lo(0)
            add_quarter(1, mixg, xT)
            scale_quarter(2, mixg)
            input_lo(1)
            add_quarter(2, mixg, xT)
            input_lo(2)

            def gate_scale(g):
                dve.wait_ge(pe_used, 8 * g + FF_C0 + 4)
                if not isinstance(g, int) or g > 0:
                    dve.wait_ge(drained[1], g + FF_G0 // 2)
                tt(sgate[:, :, :], acc(0), rbc[:, :].unsqueeze(1).broadcast_to([P, 2, T]), mul).then_inc(drained[0], 1)

            def gate_times_r(g):
                dve.wait_ge(gate_act, g + 1)
                tt(sgate[:, :, :], sgate[:, :, :], rbc[:, :].unsqueeze(1).broadcast_to([P, 2, T]), mul)\
                    .then_inc(gate_r, 1)

            def up_evac(g):
                dve.wait_ge(gate_r, g + 1)
                dve.wait_ge(pe_used, 8 * g + FF_C0 + 8)
                if not isinstance(g, int) or g > 0:
                    dve.wait_ge(nz_lo, g + 4)
                tt(hidF[:, :, :], sgate[:, :, :], acc(1), mul).then_inc(drained[1], 1)

            def hid_lo_(g):
                dve.wait_ge(ff_hi, g + 1)
                tt(hid_lo[:, ds(2 * g, 2)], hidF[:, :, :], hid_hi[:, ds(2 * g, 2)].bitcast(F32), sub).then_inc(nz_lo, 1)

            for i in range(8):
                lo(FF_C0 + i + AHEAD, (i + AHEAD) % RING)
                if i == 0:
                    input_lo(3)
                if 2 <= i <= 4:
                    dve.wait_ge(nz_sq, i)
                    if i > 2:
                        dve.wait_ge(nz_acc, i - 2)
                    tt(hF[:, 0:4], hF[:, 0:4], hF[:, 4 * i - 4:4 * i], add).then_inc(nz_acc, 1)
                if i == 6:
                    dve.wait_ge(nz_r, 2)
                    gate_scale(0)
                if i == 7:
                    gate_times_r(0)
            dve.wait_ge(tl_out, 16 * 20)
            with dve.Fori(1, FF_PAIRS) as g:
                for i in range(8):
                    lo(8 * g + FF_C0 + i + AHEAD, (i + AHEAD) % RING)
                    if i == 0:
                        up_evac(g - 1)
                    if i == 2:
                        hid_lo_(g - 1)
                    if i == 4:
                        gate_scale(g)
                    if i == 6:
                        gate_times_r(g)
            for c in range(AHEAD, DOWN_GROUPS * DOWN_CH):
                lo(DOWN_C0 + c, c % RING)
                if c == AHEAD:
                    up_evac(FF_PAIRS - 1)
                if c == AHEAD + 2:
                    hid_lo_(FF_PAIRS - 1)
                g, i = divmod(c - AHEAD, DOWN_CH)
                if i == 1 and g > 1:
                    add_squares(1, g - 1)
            add_squares(1, DOWN_GROUPS - 1)
            dve.wait_ge(o_r, 4)
            dve.wait_ge(drained[1], 44)
            for i in range(6):
                h = slice(2 * i, 2 * i + 2)
                tt(ffg[:, h], ffg[:, h], rbc[:, :].unsqueeze(1).broadcast_to([P, 2, T]), mul).then_inc(o_g, 1)
                dve.wait_ge(o_g, 3 + i)
                tt(ffg[:, h], xT[:, h], ffg[:, h], add).then_inc(o_y, 1)


_INS = ["x_prompt", "x_sample", "state_hgrn", "state_gdn", "state_gdn_conv", "state_rglru_h", "state_rglru_conv",
        "ln_mix_pre", "ln_mix_post", "ln_ffn_pre", "ln_ffn_post", "w_in", "w_out", "a_norm",
        "b_conv_w", "b_A_log", "b_dt_bias", "b_norm", "c_conv_w", "c_conv_b", "c_wa", "c_ba", "c_wx", "c_bx", "c_lam",
        "w_gate", "w_up", "w_down"]
_OUTS = [(1, 256, 2048), (8, 1, 2048), (1, 1, 4, 128, 128), (1, 8, 4, 128, 128), (1, 1, 8, 128, 128),
         (1, 8, 8, 128, 128), (1, 1, 3, 3072), (1, 8, 3, 3072), (1, 1, 512), (1, 8, 512), (1, 1, 3, 512), (1, 8, 3, 512)]


def kernel(**inputs):
    import numpy as _np
    import concourse.bacc as _bacc
    from concourse import mybir as _mybir
    from concourse.bass_utils import run_bass_kernel_spmd as _run

    nc = _bacc.Bacc("TRN2", target_bir_lowering=False, num_devices=1)
    arrays, args = {}, []
    for name in _INS:
        a = _np.ascontiguousarray(inputs[name])
        arrays[f"in_{name}_dram"] = a
        args.append(nc.dram_tensor(f"in_{name}_dram", a.shape, _mybir.dt.from_np(a.dtype), kind="ExternalInput").ap())
    for i, shape in enumerate(_OUTS):
        args.append(nc.dram_tensor(f"out_{i}_dram", shape, _mybir.dt.float32, kind="ExternalOutput").ap())
    hybrid_layer(nc, *args)
    r = _run(nc, [arrays], core_ids=[0])
    return tuple(r.results[0][f"out_{i}_dram"] for i in range(len(_OUTS)))
```
